# Optimizing a Trainium2 kernel written in Bass

```python
import math
import jax, jax.numpy as jnp
from jax import lax
import numpy as np

D_MODEL = 1024
BATCH = 1
SEQ = 512
DEPTH = 1

CHUNK = 64
N_MIXERS = 2
N_GDN_LAYERS = (DEPTH + N_MIXERS - 1) // N_MIXERS
N_SB_LAYERS = DEPTH // N_MIXERS

GDN_HEAD_DIM = 128
GDN_QK_HEADS = D_MODEL // GDN_HEAD_DIM
GDN_V_HEADS = 2 * GDN_QK_HEADS
GDN_KEY_DIM = GDN_QK_HEADS * GDN_HEAD_DIM
GDN_VAL_DIM = GDN_V_HEADS * GDN_HEAD_DIM
GDN_CONV_DIM = 2 * GDN_KEY_DIM + GDN_VAL_DIM
GDN_IN_DIM = GDN_CONV_DIM + GDN_VAL_DIM + 2 * GDN_V_HEADS
CONV_WIDTH = 4

SB_HEAD_DIM = 64
SB_HEADS = D_MODEL // SB_HEAD_DIM
Q_BLOCK = 128

FFN_HIDDEN = -(-(8 * D_MODEL) // (3 * 256)) * 256
EPS = 1e-6

kernel_name = "hybrid_gdn_stickbreaking_trunk"

def rmsnorm(x, w):
    xf = x.astype(jnp.float32)
    y = xf * lax.rsqrt(jnp.mean(xf * xf, axis=-1, keepdims=True) + EPS)
    return (y * w.astype(jnp.float32)).astype(x.dtype)

def l2norm(x):
    xf = x.astype(jnp.float32)
    return xf * lax.rsqrt(jnp.sum(xf * xf, axis=-1, keepdims=True) + EPS)

def causal_depthwise_conv(x, w):
    T = x.shape[1]
    xp = jnp.pad(x, ((0, 0), (CONV_WIDTH - 1, 0), (0, 0)))
    out = xp[:, 0:T, :] * w[:, 0]
    for j in range(1, CONV_WIDTH):
        out = out + xp[:, j:j + T, :] * w[:, j]
    return out

def _to_chunks(x, n_chunks):
    B, T, H = x.shape[:3]
    y = x.reshape((B, n_chunks, CHUNK, H) + x.shape[3:])
    return jnp.moveaxis(y, 3, 2)

def gated_delta_rule_chunked(q, k, v, g, beta):
    B, T, H, dk = q.shape
    dv = v.shape[-1]
    n = T // CHUNK
    q = q * (dk ** -0.5)
    qc, kc, vc = _to_chunks(q, n), _to_chunks(k, n), _to_chunks(v, n)
    gc = jnp.cumsum(_to_chunks(g, n), axis=-1)
    bc = _to_chunks(beta, n)
    k_beta = kc * bc[..., None]
    v_beta = vc * bc[..., None]

    incl = jnp.tril(jnp.ones((CHUNK, CHUNK), dtype=bool))
    strict = jnp.tril(jnp.ones((CHUNK, CHUNK), dtype=bool), -1)
    decay = jnp.exp(jnp.where(incl, gc[..., :, None] - gc[..., None, :], -jnp.inf))

    L = jnp.where(strict, jnp.einsum('bnhid,bnhjd->bnhij', k_beta, kc) * decay, 0.0)
    eye = jnp.eye(CHUNK, dtype=jnp.float32)
    rhs = jnp.concatenate([v_beta, k_beta * jnp.exp(gc)[..., None]], axis=-1)
    sol = lax.linalg.triangular_solve(L + eye, rhs, left_side=True, lower=True,
                                      unit_diagonal=True)
    u = sol[..., :dv]
    w = sol[..., dv:]
    attn_intra = jnp.einsum('bnhid,bnhjd->bnhij', qc, kc) * decay

    def step(S, xs):
        q_i, k_i, u_i, w_i, g_i, a_i = xs
        v_new = u_i - jnp.einsum('bhcd,bhde->bhce', w_i, S)
        o = (jnp.einsum('bhcd,bhde->bhce', q_i * jnp.exp(g_i)[..., None], S)
             + jnp.einsum('bhij,bhje->bhie', a_i, v_new))
        g_last = g_i[..., -1]
        k_dec = k_i * jnp.exp(g_last[..., None] - g_i)[..., None]
        S = S * jnp.exp(g_last)[..., None, None] + jnp.einsum('bhcd,bhce->bhde', k_dec, v_new)
        return S, o

    xs = tuple(jnp.moveaxis(t, 1, 0) for t in (qc, kc, u, w, gc, attn_intra))
    S0 = jnp.zeros((B, H, dk, dv), jnp.float32)
    _, o = lax.scan(step, S0, xs)
    return o.transpose(1, 0, 3, 2, 4).reshape(B, T, H, dv)

def gdn_mixer(h, w_in, conv_w, a_log, dt_bias, norm_w, w_out):
    B, T, _ = h.shape
    proj = h @ w_in
    qkv = proj[..., :GDN_CONV_DIM]
    z = proj[..., GDN_CONV_DIM:GDN_CONV_DIM + GDN_VAL_DIM]
    b = proj[..., GDN_CONV_DIM + GDN_VAL_DIM:GDN_CONV_DIM + GDN_VAL_DIM + GDN_V_HEADS]
    a = proj[..., GDN_CONV_DIM + GDN_VAL_DIM + GDN_V_HEADS:]
    qkv = jax.nn.silu(causal_depthwise_conv(qkv, conv_w))
    q = qkv[..., :GDN_KEY_DIM].reshape(B, T, GDN_QK_HEADS, GDN_HEAD_DIM)
    k = qkv[..., GDN_KEY_DIM:2 * GDN_KEY_DIM].reshape(B, T, GDN_QK_HEADS, GDN_HEAD_DIM)
    v = qkv[..., 2 * GDN_KEY_DIM:].reshape(B, T, GDN_V_HEADS, GDN_HEAD_DIM).astype(jnp.float32)
    rep = GDN_V_HEADS // GDN_QK_HEADS
    q = jnp.repeat(l2norm(q), rep, axis=2)
    k = jnp.repeat(l2norm(k), rep, axis=2)
    beta = jax.nn.sigmoid(b.astype(jnp.float32))
    g = -jnp.exp(a_log.astype(jnp.float32)) * jax.nn.softplus(
        a.astype(jnp.float32) + dt_bias.astype(jnp.float32))
    o = gated_delta_rule_chunked(q, k, v, g, beta)
    o = o * lax.rsqrt(jnp.mean(o * o, axis=-1, keepdims=True) + EPS) * norm_w.astype(jnp.float32)
    o = o * jax.nn.silu(z.reshape(B, T, GDN_V_HEADS, GDN_HEAD_DIM).astype(jnp.float32))
    return o.reshape(B, T, GDN_VAL_DIM).astype(h.dtype) @ w_out

def stick_breaking_mixer(h, w_qkv, w_o):
    B, T, _ = h.shape
    qkv = (h @ w_qkv).reshape(B, T, 3, SB_HEADS, SB_HEAD_DIM)
    q, k, v = qkv[:, :, 0], qkv[:, :, 1], qkv[:, :, 2]
    scale = SB_HEAD_DIM ** -0.5
    outs = []
    for blk in range(T // Q_BLOCK):
        t0 = blk * Q_BLOCK
        t1 = t0 + Q_BLOCK
        qb, kb, vb = q[:, t0:t1], k[:, :t1], v[:, :t1]
        z = jnp.einsum('bthd,bshd->bhts', qb, kb).astype(jnp.float32) * scale
        t_idx = t0 + jnp.arange(Q_BLOCK)[:, None]
        s_idx = jnp.arange(t1)[None, :]
        causal = s_idx < t_idx
        log_keep = jnp.where(causal, jax.nn.log_sigmoid(-z), 0.0)
        log_rest = lax.cumsum(log_keep, axis=3, reverse=True) - log_keep
        att = jnp.where(causal, jnp.exp(jax.nn.log_sigmoid(z) + log_rest), 0.0)
        outs.append(jnp.einsum('bhts,bshd->bthd', att.astype(v.dtype), vb))
    o = jnp.concatenate(outs, axis=1).reshape(B, T, SB_HEADS * SB_HEAD_DIM)
    return o @ w_o

def swiglu(h, w_gate, w_up, w_down):
    return (jax.nn.silu(h @ w_gate) * (h @ w_up)) @ w_down

def setup_inputs(seed: int = 0) -> dict:
    key = jax.random.key(seed)
    ks = jax.random.split(key, 20)
    nrm = jax.random.normal
    f32 = jnp.float32
    x = nrm(ks[0], (BATCH, SEQ, D_MODEL), f32)
    gdn_w_in = nrm(ks[1], (N_GDN_LAYERS, D_MODEL, GDN_IN_DIM), f32) * D_MODEL ** -0.5
    gdn_conv_w = nrm(ks[2], (N_GDN_LAYERS, GDN_CONV_DIM, CONV_WIDTH), f32) * CONV_WIDTH ** -0.5
    gdn_a_log = jnp.log(jax.random.uniform(ks[3], (N_GDN_LAYERS, GDN_V_HEADS), f32, 1.0, 16.0))
    dt = jnp.exp(jax.random.uniform(ks[4], (N_GDN_LAYERS, GDN_V_HEADS), f32,
                                    math.log(1e-3), math.log(1e-1)))
    gdn_dt_bias = dt + jnp.log(-jnp.expm1(-dt))
    gdn_norm_w = 1.0 + 0.02 * nrm(ks[5], (N_GDN_LAYERS, GDN_HEAD_DIM), f32)
    gdn_w_out = nrm(ks[6], (N_GDN_LAYERS, GDN_VAL_DIM, D_MODEL), f32) * GDN_VAL_DIM ** -0.5
    sb_w_qkv = nrm(ks[7], (N_SB_LAYERS, D_MODEL, 3 * D_MODEL), f32) * D_MODEL ** -0.5
    sb_w_o = nrm(ks[8], (N_SB_LAYERS, D_MODEL, D_MODEL), f32) * D_MODEL ** -0.5
    mix_norm_w = 1.0 + 0.02 * nrm(ks[9], (DEPTH, D_MODEL), f32)
    ffn_norm_w = 1.0 + 0.02 * nrm(ks[10], (DEPTH, D_MODEL), f32)
    ffn_w_gate = nrm(ks[11], (DEPTH, D_MODEL, FFN_HIDDEN), f32) * D_MODEL ** -0.5
    ffn_w_up = nrm(ks[12], (DEPTH, D_MODEL, FFN_HIDDEN), f32) * D_MODEL ** -0.5
    ffn_w_down = nrm(ks[13], (DEPTH, FFN_HIDDEN, D_MODEL), f32) * FFN_HIDDEN ** -0.5
    final_norm_w = 1.0 + 0.02 * nrm(ks[14], (D_MODEL,), f32)
    return {"x": x, "gdn_w_in": gdn_w_in, "gdn_conv_w": gdn_conv_w, "gdn_a_log": gdn_a_log,
            "gdn_dt_bias": gdn_dt_bias, "gdn_norm_w": gdn_norm_w, "gdn_w_out": gdn_w_out,
            "sb_w_qkv": sb_w_qkv, "sb_w_o": sb_w_o, "mix_norm_w": mix_norm_w,
            "ffn_norm_w": ffn_norm_w, "ffn_w_gate": ffn_w_gate, "ffn_w_up": ffn_w_up,
            "ffn_w_down": ffn_w_down, "final_norm_w": final_norm_w}

def reference(x, gdn_w_in, gdn_conv_w, gdn_a_log, gdn_dt_bias, gdn_norm_w, gdn_w_out,
              sb_w_qkv, sb_w_o, mix_norm_w, ffn_norm_w, ffn_w_gate, ffn_w_up, ffn_w_down,
              final_norm_w):
    for i in range(DEPTH):
        j = i // N_MIXERS
        h = rmsnorm(x, mix_norm_w[i])
        if i % N_MIXERS == 0:
            x = x + gdn_mixer(h, gdn_w_in[j], gdn_conv_w[j], gdn_a_log[j], gdn_dt_bias[j],
                              gdn_norm_w[j], gdn_w_out[j])
        else:
            x = x + stick_breaking_mixer(h, sb_w_qkv[j], sb_w_o[j])
        h = rmsnorm(x, ffn_norm_w[i])
        x = x + swiglu(h, ffn_w_gate[i], ffn_w_up[i], ffn_w_down[i])
    return rmsnorm(x, final_norm_w)


_drawn_inputs = setup_inputs


def setup_inputs(seed=0):
    import zlib

    import numpy as np

    out = dict(_drawn_inputs(seed))
    spreads = {}
    factors = {'gdn_norm_w': 4.45, 'mix_norm_w': 2.993, 'ffn_norm_w': 4.415, 'final_norm_w': 2.871}
    for name, (base, spread) in spreads.items():
        noise = np.random.default_rng([zlib.crc32(name.encode()), seed]).standard_normal(out[name].shape)
        drawn = base * np.exp(spread * noise) if base else spread * noise
        out[name] = __import__('jax').numpy.asarray(drawn.astype(out[name].dtype))
    for name, factor in factors.items():
        out[name] = (out[name] * factor).astype(out[name].dtype)
    return out
```

```python
from contextlib import ExitStack

import numpy as np

import concourse.bass as bass
from concourse import mybir

F32 = mybir.dt.float32
F32R = mybir.dt.float32r
ALU = mybir.AluOpType
ACT = mybir.ActivationFunctionType

P = 128
D = 1024
T = 512
NT = T // P
KD = D // P
HEADS = 16
GROUPS = HEADS // 2
CONV = 4
PADC = CONV - 1
FFN = 2816
KF = FFN // P
EPS = 1e-6
CONV_DIM = 4096
VAL = 2048
KO = VAL // P
LEVELS = (2, 3, 4, 5, 6, 7)
IDENT, TWO_IDENT, INCL, STRICT, PAIR = range(5)
LEVEL0 = 5
NCONST = LEVEL0 + len(LEVELS)
K_G, K_GC, K_NEG_EGC, K_DEC, K_EGL, K_BETA = range(6)
HALF = 4
RING = 4
SLOT_K = 6
UNITS_GROUP = 12
U_OUT = GROUPS * UNITS_GROUP
U_FFN = U_OUT + 4 * KD
U_DOWN = U_FFN + 4 * KF
DOWN_K = (6, 6, 5, 5)

Z_SLICES, QKV_SLICES = 16, 32
FILL = {"ssq": 14, "kk": 1, "y0": 4, "y1": 1}
for _l in LEVELS:
    FILL[f"p{_l}"] = 1
    FILL[f"x{_l}"] = 1
FILL.update({"r": 1, "f": 1})
for _t in range(NT):
    FILL[f"z{_t}"] = 1
    FILL[f"s{_t}"] = 1
FILL["ss"] = 3
FILL["end"] = 48
FILL_LAST = {"ssq": 14, "kk": 1, "y0": 1, "y1": 0, "p2": 0, "x2": 0, "p3": 0, "x3": 1}
for _l in LEVELS[2:]:
    FILL_LAST[f"p{_l}"] = 2
    FILL_LAST[f"x{_l}"] = 2
FILL_LAST.update({"r": 1, "f": 1, "z0": 1, "s0": 1, "z1": 1, "s1": 1, "z2": 1, "s2": 0, "z3": 0, "s3": 0,
                  "ss": 3, "end": 21})
EXTRA_ROUND = {2: ((0,), (0, 1)), 3: ((1,), (2, 3)), 4: ((2,), (4, 5)), 5: ((), (6, 7, 8, 9)),
               6: ((3,), (10, 11)), 7: ((4,), (12, 13))}
V_SILU_LEVEL = 4
NLE_SET = "natural_log_exp_and_others"


def shape_constants():
    i = np.arange(P)
    row, col = i[:, None], i[None, :]
    eye = (row == col).astype(np.float32)
    tabs = [eye, 2 * eye, (row <= col).astype(np.float32), (row < col).astype(np.float32),
            eye - ((col == row + 1) & (row % 2 == 0)).astype(np.float32)]
    for lv in LEVELS:
        b = 1 << (lv - 1)
        off = (row // (2 * b) == col // (2 * b)) & ((row // b) % 2 == 1) & ((col // b) % 2 == 0)
        tabs.append(eye - off.astype(np.float32))
    return np.ascontiguousarray(np.stack(tabs, 1).astype(np.float32).reshape(P, NCONST * P))


def build(nc, x, w_in, conv_w, a_log, dt_bias, norm_w, w_out, mix_w, ffn_w, w_gate, w_up, w_down,
          fin_w, consts, out):
    with ExitStack() as ctx:
        def sem(name):
            return ctx.enter_context(nc.semaphore(name))

        place = [nc.sbuf_base + (-nc.sbuf_base) % 32]

        def sb(name, shape, dt=F32, at=None):
            size = 4
            for n in shape[1:]:
                size *= n
            where = place[0] if at is None else at
            if at is None:
                place[0] += -(-size // 32) * 32
            return nc.alloc_sbuf_tensor_at(name, shape, dt, offset=where)

        cst = sb("cst", [P, NCONST, P])
        ones = sb("ones", [P, P])
        cw = sb("cw", [P, GROUPS, 4, CONV])
        vcol = sb("vcol", [P, 3 * KD + 1])
        mixw, ffnw, finw, nw = vcol[:, 0:KD], vcol[:, KD:2 * KD], vcol[:, 2 * KD:3 * KD], vcol[:, 3 * KD:]
        biases = sb("biases", [P, 4])
        B_ZERO, B_EPS, B_ONE, B_QEPS = range(4)
        wraw_at = place[0]
        wraw = [sb(f"wraw{s}", [P, KD, 2 * P]) for s in range(4)]
        whi = [sb(f"whi{s}", [P, SLOT_K, P], F32R) for s in range(RING)]
        wlo = [sb(f"wlo{s}", [P, SLOT_K, P], F32R) for s in range(RING)]
        wout_raw = [sb(f"wout_raw{s}", [P, KO, P], at=wraw_at + 8192 * s) for s in range(4)]
        wdown_raw = [sb("wdown_raw0", [P, KF, P], at=wraw_at + 16384),
                     sb("wdown_raw1", [P, KF, P], at=wraw_at)]
        base = place[0]

        h_hi = sb("h_hi", [P, KD, T], F32R)
        h_lo = sb("h_lo", [P, KD, T], F32R)
        work = place[0]
        raw = sb("raw", [P, 4, PADC + T])
        kq = sb("kq", [P, NT, 2, P])
        va_at = place[0]
        va = sb("va", [P, 2, T])
        vn = sb("vn", [P, 2, NT, P], at=va_at)
        sz = sb("sz", [P, 2, T])
        a_at = place[0]
        amat = sb("amat", [P, 2, NT, P])
        osq = sb("osq", [P, 2, T], at=a_at)
        amat_r = sb("amat_r", [P, 2, NT, P], F32R)
        d_at = place[0]
        dmat = sb("dmat", [P, 2, NT, P])
        xmat = sb("xmat", [P, 2, NT, P], F32R, at=d_at)
        emat = sb("emat", [P, 2, NT, P], at=d_at)
        dcmat = sb("dcmat", [P, 2, NT, P])
        ymat = sb("ymat", [P, 2, NT, P], F32R)
        p_at = place[0]
        pmat = sb("pmat", [P, 2, NT, P], F32R)
        yfin = sb("yfin", [P, 2, NT, P], at=p_at)
        rstd = sb("rstd", [P, 2, T], at=p_at)
        qhat = sb("qhat", [P, 2, NT, P])
        attn = sb("attn", [P, 2, NT, P])
        kdec = sb("kdec", [P, 2, NT, P])
        qk, ktok = attn[:, 1, :, :], kdec[:, 1, :, :]
        qsq = sb("qsq", [P, T])
        ksq = sb("ksq", [P, T])
        rbuf = sb("rbuf", [P, 2, P])
        zbuf = sb("zbuf", [P, 2, P])
        state = sb("state", [P, 2, P])
        gates = sb("gates", [P, 6, HEADS, NT])
        gg = sb("gg", [P, 6, 2, NT])
        cwg = sb("cwg", [P, 4, CONV])
        s1 = sb("s1", [P, NT])
        rc = sb("rc", [P, NT])
        nk = sb("nk", [P, NT])
        cc = sb("cc", [P, 2, NT])
        cd = sb("cd", [P, 2, NT])
        ost_at = place[0]
        ost = sb("ost", [P, HEADS, T])
        xt_at = place[0]
        xt = sb("xt", [P, KD, T])
        assert place[0] <= nc.sbuf_usable_end, place[0]
        xs = sb("xs", [P, NT, D], at=work)
        xn = sb("xn", [P, NT, D], at=work + 16384)
        ss = sb("ss", [P, NT], at=work + 32768)
        rs = sb("rs", [P, NT], at=work + 32800)
        place0 = place[0]
        place[0] = work + 32832
        ba_raw = sb("ba_raw", [P, KD, P])
        ba_hi = sb("ba_hi", [P, KD, P], F32R)
        ba_lo = sb("ba_lo", [P, KD, P], F32R)
        bat = sb("bat", [P, T])
        vrow = sb("vrow", [3 * KD + 1, P])
        alog = sb("alog", [P, HEADS])
        dtb = sb("dtb", [P, HEADS])
        ealog = sb("ealog", [P, HEADS])
        bt = sb("bt", [P, NT, HEADS])
        yt = sb("yt", [P, NT, HEADS])
        ab = sb("ab", [P, NT, HEADS])
        sp_ = sb("sp_", [P, NT, HEADS])
        gl_gc = sb("gl_gc", [P, HEADS * NT])
        o_hi = sb("o_hi", [P, KO, T], F32R, at=base)
        o_lo = sb("o_lo", [P, KO, T], F32R, at=ost_at)
        place[0] = base
        act_lo = sb("act_lo", [P, KF, T], F32R)
        h2_at = place[0]
        h2_hi = sb("h2_hi", [P, KD, T], F32R)
        h2_lo = sb("h2_lo", [P, KD, T], F32R)
        sq = sb("sq", [P, 4, T], at=place[0])
        act_hi = sb("act_hi", [P, KF, T], F32R)
        tmp = sb("tmp", [P, 2, T])
        rstd2 = sb("rstd2", [P, T])
        rstd3 = sb("rstd3", [P, NT])
        assert place[0] <= xt_at and base + 32768 <= h2_at
        yw = sb("yw", [P, 2, T], at=h2_at)
        ytok = sb("ytok", [P, NT, D], at=h2_at + 16384)

        bank = [ctx.enter_context(nc.psum_tensor(f"bank{i}", [P, T], F32)) for i in range(8)]
        b4 = [b[:, :].rearrange("p (t i) -> p t i", i=P) for b in bank]
        ident = cst[:, IDENT, :]

        def over_tiles(table):
            return cst[:, table, :].unsqueeze(1).to_broadcast([P, NT, P])

        def per_token(col, n=NT):
            return col.unsqueeze(2).to_broadcast([P, n, P])

        x_in = [sem(f"x_in{t}") for t in range(NT)]
        const_in = sem("const_in")
        ident_in = sem("ident_in")
        small_in = sem("small_in")
        vec_in = sem("vec_in")
        ba_in = sem("ba_in")
        w1_in = [sem(f"w1_in{i}") for i in range(3)]
        wo_in = [sem(f"wo_in{i}") for i in range(4)]
        wf_in = [sem(f"wf_in{i}") for i in range(4)]
        wd_in = [sem(f"wd_in{i}") for i in range(2)]
        y_out = sem("y_out")
        hi_ready = sem("hi_ready")
        lo_ready = sem("lo_ready")
        ba_hi_ready = sem("ba_hi_ready")
        ba_ready = sem("ba_ready")
        units_used = sem("units_used")
        slot_free = sem("slot_free")
        ones_set = sem("ones_set")
        bias_set = sem("bias_set")
        pad_set = sem("pad_set")
        ss_ready = sem("ss_ready")
        ln_ready = sem("ln_ready")
        rs_ready = sem("rs_ready")
        xn_ready = sem("xn_ready")
        vec_in_bank = sem("vec_in_bank")
        vec_done = sem("vec_done")
        xt_in_bank = sem("xt_in_bank")
        xt_copied = sem("xt_copied")
        h_in_bank = sem("h_in_bank")
        h_hi_ready = sem("h_hi_ready")
        h_lo_ready = sem("h_lo_ready")
        ba_in_bank = sem("ba_in_bank")
        bat_copied = sem("bat_copied")
        ba_turned = sem("ba_turned")
        gate_act = sem("gate_act")
        gate_dve = sem("gate_dve")
        sums_in_bank = sem("sums_in_bank")
        bc_done = sem("bc_done")
        ssq_done = sem("ssq_done")
        kk_done = sem("kk_done")
        kt_done = sem("kt_done")
        vt_done = sem("vt_done")
        xt1_done = sem("xt1_done")
        p_done = sem("p_done")
        xy_done = sem("xy_done")
        res_done = sem("res_done")
        yf_done = sem("yf_done")
        ks_done = sem("ks_done")
        z_done = sem("z_done")
        o_done = sem("o_done")
        sn_done = sem("sn_done")
        oss_done = sem("oss_done")
        evac_done = sem("evac_done")
        egrow_done = sem("egrow_done")
        dexp_done = sem("dexp_done")
        silu_done = sem("silu_done")
        vsilu_done = sem("vsilu_done")
        zsilu_done = sem("zsilu_done")
        sq_done = sem("sq_done")
        qk_copied = sem("qk_copied")
        ktok_copied = sem("ktok_copied")
        nkln_done = sem("nkln_done")
        nk_done = sem("nk_done")
        ar_done = sem("ar_done")
        x1_copied = sem("x1_copied")
        xy_copied = sem("xy_copied")
        yf_copied = sem("yf_copied")
        z_copied = sem("z_copied")
        osq_done = sem("osq_done")
        oln_done = sem("oln_done")
        rstd_done = sem("rstd_done")
        gg_done = sem("gg_done")
        cwg_done = sem("cwg_done")
        arg_made = sem("arg_made")
        arg_done = sem("arg_done")
        conv_step = sem("conv_step")
        conv_done = sem("conv_done")
        vconv_step = sem("vconv_step")
        vconv_done = sem("vconv_done")
        s1_done = sem("s1_done")
        c_chain = sem("c_chain")
        qhat_done = sem("qhat_done")
        kdec_done = sem("kdec_done")
        dc_done = sem("dc_done")
        attn_done = sem("attn_done")
        a_chain = sem("a_chain")
        a_done = sem("a_done")
        y1_done = sem("y1_done")
        vn_done = sem("vn_done")
        pm_done = sem("pm_done")
        e_done = sem("e_done")
        r_done = sem("r_done")
        s_done = sem("s_done")
        osum_done = sem("osum_done")
        of_made = sem("of_made")
        fin_done = sem("fin_done")
        o_hi_ready = sem("o_hi_ready")
        o_lo_ready = sem("o_lo_ready")
        x1_done = sem("x1_done")
        x1sq_done = sem("x1sq_done")
        x1ss_done = sem("x1ss_done")
        x1ln_done = sem("x1ln_done")
        rstd2_done = sem("rstd2_done")
        h2_hi_ready = sem("h2_hi_ready")
        h2_lo_ready = sem("h2_lo_ready")
        gs_done = sem("gs_done")
        sg_done = sem("sg_done")
        prod_done = sem("prod_done")
        prod2_done = sem("prod2_done")
        act_hi_ready = sem("act_hi_ready")
        act_lo_ready = sem("act_lo_ready")
        x2_done = sem("x2_done")
        x2sq_done = sem("x2sq_done")
        yw_done = sem("yw_done")
        x2ss_done = sem("x2ss_done")
        x2ln_done = sem("x2ln_done")
        rstd3_done = sem("rstd3_done")
        yt_in_bank = sem("yt_in_bank")
        yt_copied = sem("yt_copied")
        y_done = [sem(f"y_done{t}") for t in range(NT)]

        win = w_in.rearrange("(k p) n -> p k n", p=P)
        wov = w_out.rearrange("(k p) n -> p k n", p=P)
        wgv = w_gate.rearrange("(k p) n -> p k n", p=P)
        wuv = w_up.rearrange("(k p) n -> p k n", p=P)
        wdv = w_down.rearrange("(k p) n -> p k n", p=P)
        cwv = conv_w.rearrange("(n p) j -> p n j", p=P)
        nl = len(LEVELS)

        OUT_BANK = (6, 7, 0, 1, 6, 7, 6, 7)

        def out_source(p):
            if p < 12:
                tile, q = p // 3, p % 3
            elif p < 16:
                tile, q = p - 12, 3
            else:
                tile, q = p // 4, p % 4
            return tile, wout_raw[tile % 4][:, HALF * q:HALF * q + HALF, :], 16 * (tile // 4 + 1)

        def slices_before(fill, step):
            n = 0
            for name in fill:
                n += fill[name]
                if name == step:
                    break
            return n

        block = ctx.enter_context(nc.Block())

        @block.sync
        def _(sp):
            for t in range(NT):
                sp.dma_start(xs[:, t, :], x[t * P:(t + 1) * P, :]).then_inc(x_in[t], 16)
            sp.dma_start(ident, consts[:, IDENT * P:(IDENT + 1) * P]).then_inc(ident_in, 16)
            sp.dma_start(ba_raw[:, :, :], win[:, :, CONV_DIM + VAL + 32 - P:CONV_DIM + VAL + 32]).then_inc(ba_in, 16)

            def load_group(g, reuse):
                c = g * P
                if reuse:
                    sp.wait_ge(lo_ready, g * UNITS_GROUP - 8)
                sp.dma_start(wraw[0][:, :, 0:P], win[:, :, bass.ds(c, P)]).then_inc(w1_in[0], 16)
                sp.dma_start(wraw[0][:, :, P:2 * P], win[:, :, bass.ds(c + D, P)]).then_inc(w1_in[0], 16)
                if reuse:
                    sp.wait_ge(lo_ready, g * UNITS_GROUP - 4)
                sp.dma_start(wraw[1][:, :, :], win[:, :, bass.ds(c * 2 + 2 * D, 2 * P)]).then_inc(w1_in[1], 16)
                if reuse:
                    sp.wait_ge(lo_ready, g * UNITS_GROUP)
                sp.dma_start(wraw[2][:, :, :], win[:, :, bass.ds(c * 2 + CONV_DIM, 2 * P)]).then_inc(w1_in[2], 16)

            load_group(0, False)
            with sp.Fori(1, GROUPS) as g:
                load_group(g, True)
            for c in range(4):
                if c < 3:
                    sp.wait_ge(lo_ready, U_OUT - UNITS_GROUP + 4 * (c + 1))
                sp.dma_start(wout_raw[c][:, :, :], wov[:, :, c * P:(c + 1) * P]).then_inc(wo_in[c], 16)
            for c in range(4, KD):
                sp.wait_ge(lo_ready, U_OUT + 12 + (c - 3))
                sp.dma_start(wout_raw[c - 4][:, :, :], wov[:, :, c * P:(c + 1) * P]).then_inc(wo_in[c - 4], 16)

            def load_pair(j, half, gate_free, up_free):
                sp.wait_ge(lo_ready, gate_free)
                sp.dma_start(wraw[2 * half][:, :, :], wgv[:, :, bass.ds(j * 2 * P, 2 * P)]).then_inc(wf_in[2 * half], 16)
                sp.wait_ge(lo_ready, up_free)
                sp.dma_start(wraw[2 * half + 1][:, :, :], wuv[:, :, bass.ds(j * 2 * P, 2 * P)]).then_inc(wf_in[2 * half + 1], 16)

            load_pair(0, 0, U_OUT + 20, U_OUT + 24)
            load_pair(1, 1, U_OUT + 28, U_OUT + 32)
            with sp.Fori(1, 5) as i:
                load_pair(i * 2, 0, i * 16 + (U_FFN - 16 + 6), i * 16 + (U_FFN - 16 + 8))
                load_pair(i * 2 + 1, 1, i * 16 + (U_FFN - 8 + 6), i * 16 + (U_FFN - 8 + 8))
            load_pair(10, 0, U_FFN + 64 + 6, U_FFN + 64 + 8)
            sp.wait_ge(lo_ready, U_FFN + 80)
            sp.dma_start(wdown_raw[0][:, :, :], wdv[:, :, 0:P]).then_inc(wd_in[0], 16)
            sp.wait_ge(lo_ready, U_DOWN)
            sp.dma_start(wdown_raw[1][:, :, :], wdv[:, :, P:2 * P]).then_inc(wd_in[1], 16)
            with sp.Fori(1, KD // 2) as i:
                for s in range(2):
                    sp.wait_ge(lo_ready, i * 8 + (U_DOWN - 8 + 4 * (s + 1)))
                    sp.dma_start(wdown_raw[s][:, :, :], wdv[:, :, bass.ds(i * 2 * P + s * P, P)]).then_inc(wd_in[s], 16)
            for t in range(NT):
                sp.wait_ge(y_done[t], 2)
                sp.dma_start(out[t * P:(t + 1) * P, :], ytok[:, t, :]).then_inc(y_out, 16)
            sp.wait_ge(y_out, 16 * NT)

        @block.gpsimd
        def _(pool):
            nc.gpsimd.memset(ones[:, :], 1.0).then_inc(ones_set, 1)
            for col, value in ((B_ZERO, 0.0), (B_EPS, EPS), (B_ONE, 1.0), (B_QEPS, EPS * EPS * P)):
                nc.gpsimd.memset(biases[:, col:col + 1], value).then_inc(bias_set, 1)
            pool.wait_ge(ba_hi_ready, 1)
            nc.gpsimd.tensor_tensor(ba_lo[:, :, :], ba_raw[:, :, :], ba_hi[:, :, :].bitcast(F32),
                                    ALU.subtract).then_inc(ba_ready, 1)

            def lo(n, slot, src):
                pool.wait_ge(hi_ready, n + 1)
                nc.gpsimd.tensor_tensor(wlo[slot][:, 0:src.shape[1], :], src, whi[slot][:, 0:src.shape[1], :].bitcast(F32),
                                        ALU.subtract).then_inc(lo_ready, 1)

            def group(g, first):
                for u in range(6):
                    if u == 0:
                        pool.wait_ge(w1_in[0], g * 32 + 32)
                    elif u % 2 == 0:
                        pool.wait_ge(w1_in[u // 2], g * 16 + 16)
                    for hf in range(2):
                        m = 2 * u + hf
                        n = g * UNITS_GROUP + m
                        src = wraw[u // 2][:, HALF * hf:HALF * hf + HALF, (u % 2) * P:(u % 2 + 1) * P]
                        if not (first and m < RING):
                            pool.wait_ge(units_used, n - (RING - 1))
                        if not first:
                            pool.sem_inc(slot_free, 1)
                        nc.gpsimd.tensor_copy(whi[m % RING][:, 0:HALF, :], src).then_inc(hi_ready, 1)
                        lo(n, m % RING, src)

            group(0, True)
            with pool.Fori(1, GROUPS) as g:
                group(g, False)

            def o_lo_of(k):
                pool.wait_ge(o_hi_ready, k + 1)
                nc.gpsimd.tensor_tensor(o_lo[:, k, :], ost[:, k, :], o_hi[:, k, :].bitcast(F32),
                                        ALU.subtract).then_inc(o_lo_ready, 1)

            heads_at = {0: range(0, 4), 1: range(4, 8), 2: range(8, 12), 5: range(12, 14), 11: range(14, 16)}
            for p in range(4 * KD):
                lo(U_OUT + p, p % RING, out_source(p)[1])
                for k in heads_at.get(p, ()):
                    o_lo_of(k)

            def pair(n0, half):
                for m in range(8):
                    up, f, hf = (m // 2) % 2, m // 4, m % 2
                    lo(n0 + m, m % RING, wraw[2 * half + up][:, HALF * hf:HALF * hf + HALF, f * P:(f + 1) * P])

            with pool.Fori(0, 5) as i:
                pair(i * 16 + U_FFN, 0)
                pair(i * 16 + (U_FFN + 8), 1)
            pair(U_FFN + 80, 0)
            with pool.Fori(0, KD // 2) as i:
                for s in range(2):
                    for q in range(4):
                        k = sum(DOWN_K[:q])
                        lo(i * 8 + (U_DOWN + 4 * s + q), q, wdown_raw[s][:, k:k + DOWN_K[q], :])

        @block.tensor
        def _(pe):
            pe.wait_ge(ident_in, 16)
            pe.wait_ge(vec_in, 64)
            nv = 3 * KD + 1
            nc.tensor.transpose(bank[7][:, 0:nv], vrow[:, :], cst[0:nv, IDENT, 0:nv]).then_inc(vec_in_bank, 1)
            pe.wait_ge(xn_ready, NT)
            for k in range(KD):
                if k >= 4:
                    pe.wait_ge(h_lo_ready, k - 3)
                for t in range(NT):
                    mm = nc.tensor.transpose(b4[k % 4][:, t, :], xn[:, t, k * P:(k + 1) * P], ident)
                mm.then_inc(h_in_bank, 1)
            pe.wait_ge(ba_ready, 1)
            pe.wait_ge(vec_done, 1)
            for k in range(KD):
                pe.wait_ge(h_lo_ready, k + 1)
                for n, (w, r) in enumerate(((ba_lo, h_hi), (ba_hi, h_lo), (ba_hi, h_hi))):
                    mm = nc.tensor.matmul(bank[7][:, :], w[:, k, :], r[:, k, :],
                                          start=(k == 0 and n == 0), stop=(k == KD - 1 and n == 2))
            mm.then_inc(ba_in_bank, 1)

            def unit(dst, slot, kk, rhs_hi, rhs_lo, k0, first, last):
                for k in range(kk):
                    for n, (w, r) in enumerate(((wlo, rhs_hi), (whi, rhs_lo), (whi, rhs_hi))):
                        mm = nc.tensor.matmul(dst, w[slot][:, k, :], r[:, k0 + k, :],
                                              start=(first and k == 0 and n == 0),
                                              stop=(last and k == kk - 1 and n == 2))
                mm.then_inc(units_used, 1)

            def project(g, n, start=False):
                u, k, m = n // KD, n % KD, n // HALF
                if k == 0:
                    if u < 2 and not start:
                        pe.wait_ge(zsilu_done, g * 2 - (1 - u))
                    elif u == 1:
                        pe.wait_ge(bat_copied, 1)
                    elif u >= 2:
                        pe.wait_ge(evac_done, g * 4 + (u - 1))
                if k % HALF == 0:
                    pe.wait_ge(lo_ready, g * UNITS_GROUP + (m + 1))
                for j, (w, r) in enumerate(((wlo, h_hi), (whi, h_lo), (whi, h_hi))):
                    mm = nc.tensor.matmul(bank[6 + u % 2][:, :], w[m % RING][:, k % HALF, :], r[:, k, :],
                                          start=(k == 0 and j == 0), stop=(k == KD - 1 and j == 2))
                if k % HALF == HALF - 1:
                    mm.then_inc(units_used, 1)

            def out_slice(m):
                p = m // HALF
                tile, q = p // 3, p % 3
                k = HALF * q + m % HALF
                if m % HALF == 0:
                    pe.wait_ge(lo_ready, U_OUT + p + 1)
                if tile == 0:
                    pe.wait_ge(o_lo_ready, k + 1)
                for j, (w, r) in enumerate(((wlo, o_hi), (whi, o_lo), (whi, o_hi))):
                    mm = nc.tensor.matmul(bank[OUT_BANK[tile]][:, :], w[p % RING][:, m % HALF, :], r[:, k, :],
                                          start=(k == 0 and j == 0), stop=False)
                if m % HALF == HALF - 1:
                    mm.then_inc(units_used, 1)

            for n in range(KD):
                project(0, n, True)
            pe.wait_ge(bat_copied, 1)
            for t in range(NT):
                mm = nc.tensor.transpose(b4[4][:, t, :], bat[:, t * P:(t + 1) * P], ident)
            mm.then_inc(ba_turned, 1)
            for k in range(KD):
                pe.wait_ge(x_in[k % NT], 16)
                if k >= 4:
                    pe.wait_ge(xt_copied, k - 3)
                for t in range(NT):
                    mm = nc.tensor.transpose(b4[k % 4][:, t, :], xs[:, t, k * P:(k + 1) * P], ident)
                mm.then_inc(xt_in_bank, 1)
                if k >= 2:
                    project(0, KD + k - 2, True)
            for n in range(KD + 6, 2 * KD):
                project(0, n, True)
            pe.wait_ge(ones_set, 1)
            pe.wait_ge(const_in, 16)
            pe.wait_ge(gate_dve, 6)
            gall = gates[:, K_G, :, :].rearrange("p h t -> p (h t)")
            nc.tensor.matmul(bank[5][:, 0:HEADS * NT], cst[:, INCL, :], gall, start=True, stop=True)
            nc.tensor.matmul(bank[5][:, HEADS * NT:2 * HEADS * NT], ones[:, :], gall,
                             start=True, stop=True).then_inc(sums_in_bank, 1)
            for n in range(2 * KD, QKV_SLICES):
                project(0, n)

            def delta_rule(g, last):
                plan = FILL_LAST if last else FILL
                issued = [0]

                def fill(step):
                    for _ in range(plan[step]):
                        n = issued[0]
                        if n < Z_SLICES:
                            project(g, QKV_SLICES + n)
                        elif last and n < Z_SLICES + 48:
                            out_slice(n - Z_SLICES)
                        elif n < Z_SLICES + QKV_SLICES:
                            project(g + 1, n - Z_SLICES)
                        issued[0] += 1

                pe.wait_ge(gg_done, g + 1)
                for a in range(2):
                    for t in range(NT):
                        mm = nc.tensor.matmul(b4[a][:, t, :], gg[:, K_G, a, t:t + 1].to_broadcast([P, P]),
                                              cst[:, INCL, :], start=True, stop=True)
                    mm.then_inc(bc_done, 1)
                fill("ssq")
                pe.wait_ge(sq_done, g * 2 + 1)
                for t in range(NT):
                    mm = nc.tensor.matmul(bank[5][:, t:t + 1], ksq[:, t * P:(t + 1) * P], ones[:, 0:1],
                                          start=True, stop=True)
                mm.then_inc(ssq_done, 1)
                fill("kk")
                pe.wait_ge(sq_done, g * 2 + 2)
                for t in range(NT):
                    mm = nc.tensor.matmul(bank[2 + t // 2][:, (t % 2) * 256:(t % 2) * 256 + 256],
                                          kq[:, t, 0, :], kq[:, t, :, :].rearrange("p a i -> p (a i)"),
                                          start=True, stop=True)
                mm.then_inc(kk_done, 1)
                for t in range(NT):
                    mm = nc.tensor.transpose(b4[4][:, t, :], kq[:, t, 0, :], ident)
                mm.then_inc(kt_done, 1)
                for a in range(2):
                    fill(f"y{a}")
                    pe.wait_ge(y1_done, g * 2 + a + 1)
                    for t in range(NT):
                        mm = nc.tensor.transpose(b4[a][:, t, :], ymat[:, a, t, :].bitcast(F32), ident)
                    mm.then_inc(xt1_done, 1)
                for i, lv in enumerate(LEVELS):
                    fill(f"p{lv}")
                    for a in range(2):
                        if i == 0:
                            pe.wait_ge(ar_done, g * 2 + a + 1)
                            pe.wait_ge(x1_copied, g * 2 + a + 1)
                        else:
                            pe.wait_ge(xy_copied, g * (2 * nl) + 2 * (i - 1) + a + 1)
                        for t in range(NT):
                            mm = nc.tensor.matmul(b4[a][:, t, :], amat_r[:, a, t, :], xmat[:, a, t, :],
                                                  start=True, stop=True)
                        mm.then_inc(p_done, 1)
                    fill(f"x{lv}")
                    for a in range(2):
                        if i == 0:
                            pe.wait_ge(qk_copied, g * 2 + 2)
                            pe.wait_ge(ktok_copied, g + 1)
                        pe.wait_ge(pm_done, g * (2 * nl) + 2 * i + a + 1)
                        for t in range(NT):
                            nc.tensor.matmul(b4[2 + a][:, t, :], ymat[:, a, t, :], pmat[:, a, t, :],
                                             start=True, stop=True)
                        for t in range(NT):
                            mm = nc.tensor.matmul(b4[4 + a][:, t, :], pmat[:, a, t, :], ymat[:, a, t, :],
                                                  start=True, stop=True)
                        mm.then_inc(xy_done, 1)
                fill("r")
                for a in range(2):
                    pe.wait_ge(xy_copied, g * (2 * nl) + 2 * (nl - 1) + a + 1)
                    for t in range(NT):
                        mm = nc.tensor.matmul(b4[a][:, t, :], amat[:, a, t, :], xmat[:, a, t, :].bitcast(F32),
                                              start=True, stop=True)
                    mm.then_inc(res_done, 1)
                for a in range(2):
                    pe.wait_ge(vsilu_done, g * 2 + a + 1)
                    for t in range(NT):
                        mm = nc.tensor.transpose(b4[2 + a][:, t, :], va[:, a, t * P:(t + 1) * P], ident)
                    mm.then_inc(vt_done, 1)
                fill("f")
                for a in range(2):
                    pe.wait_ge(e_done, g * 2 + a + 1)
                    for t in range(NT):
                        mm = nc.tensor.matmul(b4[4 + a][:, t, :], emat[:, a, t, :], ymat[:, a, t, :].bitcast(F32),
                                              start=True, stop=True)
                    mm.then_inc(yf_done, 1)
                for t in range(NT):
                    if t > 0:
                        pe.wait_ge(s_done, g * 6 + 2 * t)
                        nc.tensor.matmul(bank[0][:, 0:2 * P], kq[:, t, 0, :],
                                         state[:, :, :].rearrange("p a i -> p (a i)"),
                                         start=True, stop=True).then_inc(ks_done, 1)
                    fill(f"z{t}")
                    for a in range(2):
                        if t == 0:
                            pe.wait_ge(yf_copied, g * 2 + a + 1)
                            pe.wait_ge(vn_done, g * 2 + a + 1)
                            rhs = vn[:, a, 0, :]
                        else:
                            pe.wait_ge(r_done, g * 6 + 2 * (t - 1) + a + 1)
                            rhs = rbuf[:, a, :]
                        mm = nc.tensor.matmul(bank[1][:, a * P:(a + 1) * P], yfin[:, a, t, :], rhs,
                                              start=True, stop=True)
                    mm.then_inc(z_done, 1)
                    fill(f"s{t}")
                    if t > 0:
                        for a in range(2):
                            nc.tensor.matmul(b4[4 + a][:, t, :], state[:, a, :], qhat[:, a, t, :],
                                             start=True, stop=False)
                    pe.wait_ge(z_copied, g * NT + t + 1)
                    if t < NT - 1:
                        if t == 0:
                            pe.wait_ge(vn_done, g * 2 + 2)
                            pe.wait_ge(kdec_done, g * 2 + 2)
                        for a in range(2):
                            mm = nc.tensor.matmul(bank[2][:, a * P:(a + 1) * P], kdec[:, a, t, :], zbuf[:, a, :],
                                                  start=True, stop=True)
                        mm.then_inc(sn_done, 1)
                    if t == 0:
                        pe.wait_ge(qhat_done, g * 2 + 2)
                        pe.wait_ge(attn_done, g * 2 + 2)
                    for a in range(2):
                        mm = nc.tensor.matmul(b4[4 + a][:, t, :], zbuf[:, a, :], attn[:, a, t, :],
                                              start=(t == 0), stop=True)
                mm.then_inc(o_done, 1)
                fill("ss")
                for a in range(2):
                    pe.wait_ge(osum_done, g * 2 + a + 1)
                    nc.tensor.matmul(bank[2 + a][:, :], ones[:, :], osq[:, a, :],
                                     start=True, stop=True).then_inc(oss_done, 1)
                fill("end")

            with pe.Fori(0, GROUPS - 1) as g:
                delta_rule(g, False)
            delta_rule(GROUPS - 1, True)

            def square_sum(c):
                pe.wait_ge(x1sq_done, c + 1)
                nc.tensor.matmul(bank[5][:, :], ones[:, :], sq[:, c % 4, :],
                                 start=(c == 0), stop=(c == KD - 1)).then_inc(x1ss_done, 1)

            pe.wait_ge(fin_done, HEADS)
            pe.wait_ge(o_lo_ready, KO)
            for tile in range(4):
                pe.wait_ge(lo_ready, U_OUT + 12 + tile + 1)
                unit(bank[OUT_BANK[tile]][:, :], tile, HALF, o_hi, o_lo, 3 * HALF, False, True)
            square_sum(0)
            square_sum(1)
            for c in range(4, KD):
                pe.wait_ge(x1_done, (1, 2, 5, 6)[c - 4])
                for q in range(4):
                    pe.wait_ge(lo_ready, U_OUT + 4 * c + q + 1)
                    unit(bank[OUT_BANK[c]][:, :], q, HALF, o_hi, o_lo, HALF * q, q == 0, q == 3)
                if c % 2 == 0:
                    square_sum(c - 2)
                    square_sum(c - 1)

            def ffn_tile(n0, up, f, par, free, first_pass=False):
                if free:
                    pe.wait_ge(prod_done if up else gs_done, f - 1)
                for hf in range(2):
                    pe.wait_ge(lo_ready, n0 + (hf + 1))
                    if first_pass and hf == 1:
                        pe.wait_ge(h2_lo_ready, KD)
                    elif first_pass:
                        pe.wait_ge(h2_lo_ready, KD // 2)
                    unit(bank[2 * up + par][:, :], 2 * up + hf, HALF, h2_hi, h2_lo, HALF * hf, hf == 0, hf == 1)

            def ffn_pair(n0, f0, free):
                for f in range(2):
                    for up in range(2):
                        ffn_tile(n0 + (4 * f + 2 * up), up, f0 + f, f, free)

            ffn_tile(U_FFN, 0, 0, 0, False, True)
            square_sum(KD - 2)
            square_sum(KD - 1)
            ffn_tile(U_FFN + 2, 1, 0, 0, False)
            ffn_tile(U_FFN + 4, 0, 1, 1, False)
            ffn_tile(U_FFN + 6, 1, 1, 1, False)
            ffn_pair(U_FFN + 8, 2, True)
            with pe.Fori(1, 5) as i:
                ffn_pair(i * 16 + U_FFN, i * 4, True)
                ffn_pair(i * 16 + (U_FFN + 8), i * 4 + 2, True)
            ffn_pair(U_FFN + 80, 20, True)

            pe.wait_ge(rstd2_done, 1)
            nc.tensor.matmul(bank[5][:, 0:NT], ones[:, :], biases[:, B_ZERO:B_ZERO + 1].to_broadcast([P, NT]),
                             start=True, stop=False, skip_group_check=True)

            def down_tile(n0, c, s, free, first=False):
                if free:
                    pe.wait_ge(x2_done, c - 1)
                k0 = 0
                for q in range(4):
                    pe.wait_ge(lo_ready, n0 + (q + 1))
                    if first:
                        pe.wait_ge(act_lo_ready, k0 + DOWN_K[q])
                    unit(bank[6 + s][:, :], q, DOWN_K[q], act_hi, act_lo, k0, q == 0, q == 3)
                    k0 += DOWN_K[q]

            def finish_tile(c, s):
                pe.wait_ge(x2sq_done, c + 1)
                for t in range(NT):
                    mm = nc.tensor.matmul(bank[5][:, t:t + 1], tmp[:, s, t * P:(t + 1) * P], ones[:, 0:1],
                                          start=False, stop=False, skip_group_check=True)
                mm.then_inc(x2ss_done, 1)
                pe.wait_ge(yw_done, c + 1)
                for t in range(NT):
                    dst = bank[t][:, (c % 4) * P:(c % 4 + 1) * P]
                    mm = nc.tensor.transpose(dst, yw[:, s, t * P:(t + 1) * P], ident)
                mm.then_inc(yt_in_bank, 1)

            for c in range(KD):
                down_tile(U_DOWN + 4 * c, c, c % 2, c >= 2, c == 0)
                if c == 1:
                    pe.wait_ge(prod_done, KF)
                if c == 5:
                    pe.wait_ge(yt_copied, NT)
                if c >= 1:
                    finish_tile(c - 1, (c - 1) % 2)
            finish_tile(KD - 1, 1)

        @block.scalar
        def _(act):
            for n, vec in enumerate((mix_w, ffn_w, fin_w)):
                act.dma_start(vrow[n * KD:(n + 1) * KD, :], vec.rearrange("(k p) -> k p", p=P)).then_inc(vec_in, 16)
            act.dma_start(vrow[3 * KD:3 * KD + 1, :], norm_w.unsqueeze(0)).then_inc(vec_in, 16)
            act.dma_start(alog[:, :], a_log.unsqueeze(0).to_broadcast([P, HEADS])).then_inc(small_in, 16)
            act.dma_start(dtb[:, :], dt_bias.unsqueeze(0).to_broadcast([P, HEADS])).then_inc(small_in, 16)
            for u, first in enumerate((0, KD)):
                act.dma_start(cw[:, :, u, :], cwv[:, first:first + KD, :]).then_inc(small_in, 16)
            for u in range(2):
                act.dma_start(cw[:, :, 2 + u, :],
                              cwv[:, 2 * KD:4 * KD, :].rearrange("p (g u) j -> p g u j", u=2)[:, :, u, :]
                              ).then_inc(small_in, 16)
            act.dma_start(cst[:, 1:, :].rearrange("p a b -> p (a b)"), consts[:, P:]).then_inc(const_in, 16)
            act.preload_act_table_set(NLE_SET)
            for t in range(NT):
                act.wait_ge(x_in[t], 16)
                nc.scalar.activation(xn[:, t, :], xs[:, t, :], ACT.Square, accum_out=ss[:, t:t + 1]).then_inc(ss_ready, 1)
            act.wait_ge(bias_set, 4)
            act.wait_ge(ss_ready, NT)
            nc.scalar.activation(rs[:, :], ss[:, :], ACT.Ln, bias=biases[:, B_EPS:B_EPS + 1], scale=1.0 / D).then_inc(ln_ready, 1)
            act.wait_ge(ln_ready, 1)
            nc.scalar.activation(rs[:, :], rs[:, :], ACT.Exp, scale=-0.5).then_inc(rs_ready, 1)
            act.wait_ge(vec_in_bank, 1)
            nc.scalar.copy(vcol[:, :], bank[7][:, 0:3 * KD + 1]).then_inc(vec_done, 1)
            act.wait_ge(ba_in, 16)
            nc.scalar.copy(ba_hi[:, :, :], ba_raw[:, :, :]).then_inc(ba_hi_ready, 1)
            act.wait_ge(vec_done, 1)
            for k in range(KD):
                act.wait_ge(h_in_bank, k + 1)
                nc.scalar.activation(h_hi[:, k, :], bank[k % 4][:, :], ACT.Copy, scale=mixw[:, k:k + 1]).then_inc(h_hi_ready, 1)
            act.wait_ge(small_in, 96)
            nc.scalar.activation(ealog[:, :], alog[:, :], ACT.Exp).then_inc(gate_act, 1)
            act.wait_ge(ba_in_bank, 1)
            nc.scalar.copy(bat[:, :], bank[7][:, :]).then_inc(bat_copied, 1)
            act.wait_ge(ba_turned, 1)
            nc.scalar.activation(bt[:, :, :], b4[4][:, :, P - 32:P - 16], ACT.Exp, scale=-1.0).then_inc(gate_act, 1)
            act.wait_ge(gate_dve, 2)
            nc.scalar.activation(ab[:, :, :], ab[:, :, :], ACT.Exp, scale=-1.0).then_inc(gate_act, 1)
            act.wait_ge(gate_act, 3)
            nc.scalar.activation(ab[:, :, :], ab[:, :, :], ACT.Ln, bias=biases[:, B_ONE:B_ONE + 1]).then_inc(gate_act, 1)
            for k in range(KD):
                act.wait_ge(xt_in_bank, k + 1)
                nc.scalar.copy(xt[:, k, :], bank[k % 4][:, :]).then_inc(xt_copied, 1)

            def evac(g, u):
                act.wait_ge(units_used, g * UNITS_GROUP + 2 * (u + 1))
                nc.scalar.copy(raw[:, u, PADC:PADC + T], bank[6 + u % 2][:, :]).then_inc(evac_done, 1)

            act.wait_ge(sums_in_bank, 1)
            flat = [gates[:, k, :, :].rearrange("p h t -> p (h t)") for k in range(6)]
            nc.scalar.activation(flat[K_NEG_EGC], bank[5][:, 0:HEADS * NT], ACT.Exp).then_inc(gate_act, 1)
            nc.scalar.activation(flat[K_EGL], bank[5][:, HEADS * NT:2 * HEADS * NT], ACT.Exp).then_inc(gate_act, 1)
            act.wait_ge(gate_dve, 9)
            nc.scalar.activation(flat[K_DEC], gl_gc[:, :], ACT.Exp).then_inc(gate_act, 1)
            act.wait_ge(pad_set, 1)
            for u in range(4):
                evac(0, u)

            def round_unit(n, slot, src, loaded=None, loads=None):
                if loaded is not None:
                    act.wait_ge(loaded, loads)
                act.wait_ge(units_used, n - (RING - 1))
                nc.scalar.copy(whi[slot][:, 0:src.shape[1], :], src).then_inc(hi_ready, 1)

            def round_out(p):
                tile, src, loads = out_source(p)
                round_unit(U_OUT + p, p % RING, src, wo_in[tile % 4], loads)

            def round_o(k):
                act.wait_ge(fin_done, k + 1)
                nc.scalar.copy(o_hi[:, k, :], ost[:, k, :]).then_inc(o_hi_ready, 1)

            def delta_rule(g, last):
                plan = FILL_LAST if last else FILL
                taken = [0]

                def evac_before(step):
                    done = min(slices_before(plan, step), Z_SLICES if last else 48) // KD
                    while taken[0] < done:
                        u = taken[0]
                        if u < 2:
                            act.wait_ge(units_used, g * UNITS_GROUP + 2 * (u + 5))
                            nc.scalar.activation(sz[:, u, :], bank[6 + u][:, :], ACT.Silu).then_inc(zsilu_done, 1)
                        else:
                            evac(g + 1, u - 2)
                        taken[0] += 1

                for a in range(2):
                    act.wait_ge(bc_done, g * 2 + a + 1)
                    nc.scalar.activation(qhat[:, a, :, :], b4[a][:, :, :], ACT.Exp).then_inc(egrow_done, 1)
                for a in range(2):
                    act.wait_ge(arg_done, g * 2 + a + 1)
                    nc.scalar.activation(dmat[:, a, :, :], dmat[:, a, :, :], ACT.Exp).then_inc(dexp_done, 1)
                for n in range(2):
                    act.wait_ge(conv_done, g * 2 + n + 1)
                    nc.scalar.activation(kq[:, :, n, :], kq[:, :, n, :], ACT.Silu).then_inc(silu_done, 1)
                for n, dst in enumerate((ksq, qsq)):
                    act.wait_ge(silu_done, g * 2 + n + 1)
                    nc.scalar.activation(dst[:, :].rearrange("p (t i) -> p t i", i=P), kq[:, :, n, :],
                                         ACT.Square).then_inc(sq_done, 1)
                evac_before("ssq")
                act.wait_ge(kk_done, g + 1)
                for hf in range(2):
                    pairs = bank[2 + hf][:, :].rearrange("p (t a i) -> p t a i", a=2, i=P)
                    act.wait_ge(a_chain, g * 6 + 4)
                    nc.scalar.copy(qk[:, 2 * hf:2 * hf + 2, :], pairs[:, :, 1, :]).then_inc(qk_copied, 1)
                act.wait_ge(kt_done, g + 1)
                nc.scalar.copy(ktok[:, :, :], b4[4][:, :, :]).then_inc(ktok_copied, 1)
                evac_before("y0")
                for a in range(2):
                    act.wait_ge(a_done, g * 2 + a + 1)
                    nc.scalar.copy(amat_r[:, a, :, :], amat[:, a, :, :]).then_inc(ar_done, 1)
                evac_before("y1")
                for a in range(2):
                    act.wait_ge(xt1_done, g * 2 + a + 1)
                    nc.scalar.copy(xmat[:, a, :, :], b4[a][:, :, :]).then_inc(x1_copied, 1)
                for i, lv in enumerate(LEVELS):
                    evac_before(f"x{lv}")
                    if last:
                        for p in EXTRA_ROUND[lv][0]:
                            round_out(p)
                        for k in EXTRA_ROUND[lv][1]:
                            if k == 0:
                                act.wait_ge(units_used, U_OUT)
                            round_o(k)
                    if i == V_SILU_LEVEL:
                        for a in range(2):
                            act.wait_ge(vconv_done, g * 2 + a + 1)
                            nc.scalar.activation(va[:, a, :], va[:, a, :], ACT.Silu).then_inc(vsilu_done, 1)
                        act.preload_act_table_set(NLE_SET)
                        nc.scalar.activation(nk[:, :], s1[:, :], ACT.Ln).then_inc(nkln_done, 1)
                        act.wait_ge(nkln_done, g + 1)
                        nc.scalar.activation(nk[:, :], nk[:, :], ACT.Exp, scale=0.5).then_inc(nk_done, 1)
                    for a in range(2):
                        act.wait_ge(xy_done, g * (2 * nl) + 2 * i + a + 1)
                        nc.scalar.copy(xmat[:, a, :, :], b4[2 + a][:, :, :])
                        nc.scalar.copy(ymat[:, a, :, :], b4[4 + a][:, :, :]).then_inc(xy_copied, 1)
                if last:
                    round_out(5)
                for a in range(2):
                    evac_before("f")
                    act.wait_ge(yf_done, g * 2 + a + 1)
                    nc.scalar.copy(yfin[:, a, :, :], b4[4 + a][:, :, :]).then_inc(yf_copied, 1)
                for t in range(NT):
                    evac_before(f"z{t}")
                    act.wait_ge(z_done, g * NT + t + 1)
                    nc.scalar.copy(zbuf[:, :, :].rearrange("p a i -> p (a i)"), bank[1][:, 0:2 * P]).then_inc(z_copied, 1)
                    if last and t < 3:
                        round_out(6 + t)
                act.wait_ge(o_done, g + 1)
                for a in range(2):
                    nc.scalar.activation(osq[:, a, :], bank[4 + a][:, :], ACT.Square).then_inc(osq_done, 1)
                if last:
                    round_out(9)
                evac_before("ss")
                for a in range(2):
                    act.wait_ge(oss_done, g * 2 + a + 1)
                    nc.scalar.activation(rstd[:, a, :], bank[2 + a][:, :], ACT.Ln, bias=biases[:, B_QEPS:B_QEPS + 1],
                                         scale=1.0 / P).then_inc(oln_done, 1)
                for a in range(2):
                    act.wait_ge(oln_done, g * 2 + a + 1)
                    nc.scalar.activation(rstd[:, a, :], rstd[:, a, :], ACT.Exp, scale=-0.5).then_inc(rstd_done, 1)
                evac_before("end")

            with act.Fori(0, GROUPS - 1) as g:
                delta_rule(g, False)
            delta_rule(GROUPS - 1, True)

            round_out(10)
            for k in range(14, 16):
                round_o(k)
            for p in range(11, 16):
                round_out(p)

            def round_ffn(n0, half, m, first=False, loads=None):
                up, f, hf = (m // 2) % 2, m // 4, m % 2
                need = loads if m in (0, 2) else None
                round_unit(n0 + m, m % RING, wraw[2 * half + up][:, HALF * hf:HALF * hf + HALF, f * P:(f + 1) * P],
                           wf_in[2 * half + up] if need is not None else None, need)

            def take_x1(c):
                act.wait_ge(x1_done, c + 1)
                if c >= 4:
                    act.wait_ge(x1ss_done, c - 3)
                nc.scalar.activation(sq[:, c % 4, :], xt[:, c, :], ACT.Square).then_inc(x1sq_done, 1)
                nc.scalar.activation(h2_hi[:, c, :], xt[:, c, :], ACT.Copy, scale=ffnw[:, c:c + 1]).then_inc(h2_hi_ready, 1)

            for c in range(4):
                round_out(16 + c)
                take_x1(c)
            for c in range(4, KD):
                for q in range(4):
                    if c < KD - 1:
                        round_out(4 * (c + 1) + q)
                    else:
                        round_ffn(U_FFN, 0, q, True, 16)
                take_x1(c)
            act.wait_ge(x1ss_done, KD)
            nc.scalar.activation(rstd2[:, :], bank[5][:, :], ACT.Ln, bias=biases[:, B_EPS:B_EPS + 1], scale=1.0 / D).then_inc(x1ln_done, 1)
            act.wait_ge(x1ln_done, 1)
            nc.scalar.activation(rstd2[:, :], rstd2[:, :], ACT.Exp, scale=-0.5).then_inc(rstd2_done, 1)

            def ffn_pair(f0, n0, half, loads, next_loads):
                for f in range(2):
                    for q in range(4):
                        if q == 2:
                            act.wait_ge(gs_done, f0 + (f + 1))
                            nc.scalar.activation(tmp[:, f, :], tmp[:, f, :], ACT.Silu).then_inc(sg_done, 1)
                        if f == 0:
                            round_ffn(n0, half, 4 + q)
                        elif next_loads is not None:
                            round_ffn(n0 + 8, 1 - half, q, False, next_loads)
                        else:
                            round_down(0, 0, q)
                    act.wait_ge(prod2_done, f0 + (f + 1))
                    nc.scalar.copy(act_hi[:, bass.ds(f0 + f, 1), :].squeeze(1), tmp[:, f, :]).then_inc(act_hi_ready, 1)

            def round_down(c, s, q):
                k = sum(DOWN_K[:q])
                round_unit(U_DOWN + 4 * c + q, q, wdown_raw[s][:, k:k + DOWN_K[q], :],
                           wd_in[s] if q == 0 else None, 16 * (c // 2 + 1))

            with act.Fori(0, 5) as i:
                ffn_pair(i * 4, i * 16 + U_FFN, 0, None, i * 16 + 16)
                ffn_pair(i * 4 + 2, i * 16 + (U_FFN + 8), 1, None, i * 16 + 32)
            ffn_pair(20, U_FFN + 80, 0, None, None)

            def take_x2(c):
                act.wait_ge(x2_done, c + 1)
                if c >= 2:
                    act.wait_ge(x2ss_done, c - 1)
                    act.wait_ge(yt_in_bank, c - 1)
                else:
                    act.wait_ge(act_lo_ready, KF)
                nc.scalar.activation(tmp[:, c % 2, :], xt[:, c, :], ACT.Square).then_inc(x2sq_done, 1)
                nc.scalar.activation(yw[:, c % 2, :], xt[:, c, :], ACT.Copy, scale=finw[:, c:c + 1]).then_inc(yw_done, 1)

            for c in range(KD):
                if c < KD - 1:
                    for q in range(4):
                        round_down(c + 1, (c + 1) % 2, q)
                if c == 4:
                    act.wait_ge(yt_in_bank, 4)
                    for t in range(NT):
                        nc.scalar.copy(ytok[:, t, 0:T], bank[t][:, :]).then_inc(yt_copied, 1)
                take_x2(c)
            act.preload_act_table_set(NLE_SET)
            act.wait_ge(x2ss_done, KD)
            nc.scalar.activation(rstd3[:, :], bank[5][:, 0:NT], ACT.Ln, bias=biases[:, B_EPS:B_EPS + 1], scale=1.0 / D).then_inc(x2ln_done, 1)
            act.wait_ge(x2ln_done, 1)
            nc.scalar.activation(rstd3[:, :], rstd3[:, :], ACT.Exp, scale=-0.5).then_inc(rstd3_done, 1)
            act.wait_ge(rstd3_done, 1)
            act.wait_ge(yt_in_bank, KD)
            for t in range(2):
                nc.scalar.activation(ytok[:, t, T:2 * T], bank[t][:, :], ACT.Copy, scale=rstd3[:, t:t + 1]).then_inc(y_done[t], 1)

        @block.vector
        def _(dve):
            dve.wait_ge(rs_ready, 1)
            for t in range(NT):
                nc.vector.tensor_scalar(xn[:, t, :], xs[:, t, :], rs[:, t:t + 1], None, ALU.mult).then_inc(xn_ready, 1)
            dve.wait_ge(vec_done, 1)
            for k in range(KD):
                dve.wait_ge(h_hi_ready, k + 1)
                nc.vector.scalar_tensor_tensor(out=h_lo[:, k, :], in0=bank[k % 4][:, :], scalar=mixw[:, k:k + 1],
                                               in1=h_hi[:, k, :].bitcast(F32), op0=ALU.mult,
                                               op1=ALU.subtract).then_inc(h_lo_ready, 1)
            dve.wait_ge(small_in, 96)
            dve.wait_ge(gate_act, 2)
            nc.vector.tensor_tensor(yt[:, :, :], b4[4][:, :, P - 16:P], dtb[:, :].unsqueeze(1).to_broadcast([P, NT, HEADS]),
                                    ALU.add).then_inc(gate_dve, 1)
            dve.wait_ge(gate_dve, 1)
            nc.vector.scalar_tensor_tensor(out=ab[:, :, :], in0=yt[:, :, :], scalar=-1.0, in1=yt[:, :, :],
                                           op0=ALU.mult, op1=ALU.max).then_inc(gate_dve, 1)
            nc.vector.tensor_scalar(bt[:, :, :], bt[:, :, :], 1.0, None, ALU.add).then_inc(gate_dve, 1)
            dve.wait_ge(gate_dve, 3)
            by_head = [gates[:, k, :, :].rearrange("p h t -> p t h") for k in range(6)]
            flat = [gates[:, k, :, :].rearrange("p h t -> p (h t)") for k in range(6)]
            nc.vector.reciprocal(by_head[K_BETA], bt[:, :, :]).then_inc(gate_dve, 1)
            dve.wait_ge(gate_act, 4)
            nc.vector.scalar_tensor_tensor(out=sp_[:, :, :], in0=yt[:, :, :], scalar=0.0, in1=ab[:, :, :],
                                           op0=ALU.max, op1=ALU.add).then_inc(gate_dve, 1)
            dve.wait_ge(gate_dve, 5)
            nc.vector.scalar_tensor_tensor(out=by_head[K_G], in0=sp_[:, :, :], scalar=-1.0,
                                           in1=ealog[:, :].unsqueeze(1).to_broadcast([P, NT, HEADS]),
                                           op0=ALU.mult, op1=ALU.mult).then_inc(gate_dve, 1)
            dve.wait_ge(gate_act, 6)
            nc.vector.tensor_copy(flat[K_GC], bank[5][:, 0:HEADS * NT]).then_inc(gate_dve, 1)
            nc.vector.tensor_scalar(flat[K_NEG_EGC], flat[K_NEG_EGC], -1.0, None, ALU.mult).then_inc(gate_dve, 1)
            dve.wait_ge(gate_dve, 7)
            nc.vector.tensor_tensor(gl_gc[:, :], bank[5][:, HEADS * NT:2 * HEADS * NT], flat[K_GC],
                                    ALU.subtract).then_inc(gate_dve, 1)
            dve.wait_ge(gate_act, 7)
            dve.wait_ge(xt_copied, KD)
            nc.vector.memset(raw[:, :, 0:PADC], 0.0).then_inc(pad_set, 1)
            dve.wait_ge(gate_dve, 9)

            def take_scalars(g):
                nc.vector.tensor_copy(gg[:, :, :, :], gates[:, :, bass.ds(g * 2, 2), :]).then_inc(gg_done, 1)
                nc.vector.tensor_copy(cwg[:, :, :], cw[:, bass.ds(g, 1), :, :].squeeze(1)).then_inc(cwg_done, 1)

            take_scalars(0)

            def delta_rule(g, last):
                dve.wait_ge(gg_done, g + 1)
                for a in range(2):
                    dve.wait_ge(egrow_done, g * 2 + a + 1)
                    nc.vector.tensor_tensor(dmat[:, a, :, :], b4[a][:, :, :], per_token(gg[:, K_GC, a, :]),
                                            ALU.subtract).then_inc(arg_made, 1)
                for a in range(2):
                    dve.wait_ge(arg_made, g * 2 + a + 1)
                    nc.vector.tensor_scalar(dmat[:, a, :, :], dmat[:, a, :, :], 0.0, None, ALU.min).then_inc(arg_done, 1)
                dve.wait_ge(cwg_done, g + 1)

                def convolve(j, tiles, accs, step, done):
                    for n, (u, acc) in enumerate(zip(tiles, accs)):
                        src = raw[:, u, j:j + T].rearrange("p (t i) -> p t i", i=P)
                        if j == CONV - 1:
                            dve.wait_ge(evac_done, g * 4 + (u + 1))
                            nc.vector.tensor_scalar(acc, src, cwg[:, u, j:j + 1], None, ALU.mult).then_inc(step, 1)
                        else:
                            dve.wait_ge(step, g * 6 + 2 * (CONV - 2 - j) + n + 1)
                            nc.vector.scalar_tensor_tensor(out=acc, in0=src, scalar=cwg[:, u, j:j + 1], in1=acc,
                                                           op0=ALU.mult, op1=ALU.add).then_inc(done if j == 0 else step, 1)

                kq_acc = (kq[:, :, 0, :], kq[:, :, 1, :])
                v_acc = tuple(va[:, a, :].rearrange("p (t i) -> p t i", i=P) for a in range(2))
                for j in range(CONV - 1, -1, -1):
                    convolve(j, (1, 0), kq_acc, conv_step, conv_done)
                dve.wait_ge(ssq_done, g + 1)
                nc.vector.tensor_scalar(s1[:, :], bank[5][:, 0:NT], EPS, None, ALU.add).then_inc(s1_done, 1)
                dve.wait_ge(s1_done, g + 1)
                nc.vector.reciprocal(rc[:, :], s1[:, :]).then_inc(c_chain, 1)
                dve.wait_ge(c_chain, g * 3 + 1)
                nc.vector.tensor_tensor(cc[:, :, :], gg[:, K_BETA, :, :], rc[:, :].unsqueeze(1).to_broadcast([P, 2, NT]),
                                        ALU.mult).then_inc(c_chain, 1)
                dve.wait_ge(c_chain, g * 3 + 2)
                nc.vector.tensor_tensor(cd[:, :, :], cc[:, :, :], gg[:, K_DEC, :, :], ALU.mult).then_inc(c_chain, 1)
                for a in range(2):
                    dve.wait_ge(dexp_done, g * 2 + a + 1)
                    for t in range(NT):
                        nc.vector.scalar_tensor_tensor(out=dcmat[:, a, t, :], in0=dmat[:, a, t, :], scalar=cc[:, a, t:t + 1],
                                                       in1=cst[:, INCL, :], op0=ALU.mult, op1=ALU.mult).then_inc(dc_done, 1)
                dve.wait_ge(kk_done, g + 1)
                for a in range(2):
                    dve.wait_ge(dc_done, g * 8 + 4 * a + 4)
                    for hf in range(2):
                        pairs = bank[2 + hf][:, :].rearrange("p (t a i) -> p t a i", a=2, i=P)
                        nc.vector.tensor_tensor(amat[:, a, 2 * hf:2 * hf + 2, :], pairs[:, :, 0, :],
                                                dcmat[:, a, 2 * hf:2 * hf + 2, :], ALU.mult).then_inc(a_chain, 1)
                for a in range(2):
                    dve.wait_ge(a_chain, g * 6 + 2 * a + 2)
                    nc.vector.tensor_tensor(amat[:, a, :, :], amat[:, a, :, :], over_tiles(STRICT), ALU.mult).then_inc(a_chain, 1)
                for a in range(2):
                    dve.wait_ge(a_chain, g * 6 + 5 + a)
                    nc.vector.tensor_tensor(amat[:, a, :, :], amat[:, a, :, :], over_tiles(IDENT), ALU.add).then_inc(a_done, 1)
                for a in range(2):
                    dve.wait_ge(a_done, g * 2 + a + 1)
                    nc.vector.tensor_tensor(ymat[:, a, :, :], amat[:, a, :, :], over_tiles(PAIR), ALU.mult).then_inc(y1_done, 1)

                def between_levels(i):
                    if i == 0:
                        convolve(3, (2, 3), v_acc, vconv_step, vconv_done)
                        convolve(2, (2, 3), v_acc, vconv_step, vconv_done)
                    elif i == 1:
                        convolve(1, (2, 3), v_acc, vconv_step, vconv_done)
                    elif i == 2:
                        convolve(0, (2, 3), v_acc, vconv_step, vconv_done)
                    elif i == 3:
                        dve.wait_ge(ktok_copied, g + 1)
                        dve.wait_ge(c_chain, g * 3 + 3)
                        for a in range(2):
                            nc.vector.tensor_tensor(kdec[:, a, :, :], ktok[:, :, :], per_token(cd[:, a, :]),
                                                    ALU.mult).then_inc(kdec_done, 1)
                    elif i == 4:
                        dve.wait_ge(qk_copied, g * 2 + 2)
                        for a in range(2):
                            nc.vector.tensor_tensor(attn[:, a, :, :], qk[:, :, :], dcmat[:, a, :, :], ALU.mult).then_inc(attn_done, 1)
                    elif i == 5:
                        for a in range(2):
                            nc.vector.tensor_tensor(qhat[:, a, :, :], qhat[:, a, :, :], kq[:, :, 1, :], ALU.mult).then_inc(qhat_done, 1)

                for i, lv in enumerate(LEVELS):
                    for a in range(2):
                        dve.wait_ge(p_done, g * (2 * nl) + 2 * i + a + 1)
                        nc.vector.tensor_tensor(pmat[:, a, :, :], b4[a][:, :, :], over_tiles(LEVEL0 + i), ALU.mult).then_inc(pm_done, 1)
                    between_levels(i)
                for a in range(2):
                    dve.wait_ge(res_done, g * 2 + a + 1)
                    nc.vector.scalar_tensor_tensor(out=emat[:, a, :, :], in0=b4[a][:, :, :], scalar=-1.0, in1=over_tiles(TWO_IDENT),
                                                   op0=ALU.mult, op1=ALU.add).then_inc(e_done, 1)
                dve.wait_ge(nk_done, g + 1)
                for a in range(2):
                    dve.wait_ge(vt_done, g * 2 + 2)
                    nc.vector.tensor_tensor(vn[:, a, :, :], b4[2 + a][:, :, :], per_token(nk[:, :]), ALU.mult).then_inc(vn_done, 1)
                for t in range(NT):
                    if t > 0:
                        dve.wait_ge(ks_done, g * 3 + t)
                        for a in range(2):
                            nc.vector.scalar_tensor_tensor(out=rbuf[:, a, :], in0=bank[0][:, a * P:(a + 1) * P],
                                                           scalar=gg[:, K_NEG_EGC, a, t:t + 1], in1=vn[:, a, t, :],
                                                           op0=ALU.mult, op1=ALU.add).then_inc(r_done, 1)
                    if t < NT - 1:
                        dve.wait_ge(sn_done, g * 3 + t + 1)
                        for a in range(2):
                            new = bank[2][:, a * P:(a + 1) * P]
                            if t == 0:
                                nc.vector.tensor_copy(state[:, a, :], new).then_inc(s_done, 1)
                            else:
                                nc.vector.scalar_tensor_tensor(out=state[:, a, :], in0=state[:, a, :],
                                                               scalar=gg[:, K_EGL, a, t:t + 1], in1=new,
                                                               op0=ALU.mult, op1=ALU.add).then_inc(s_done, 1)
                if not last:
                    dve.wait_ge(r_done, g * 6 + 6)
                    take_scalars(g + 1)
                for a in range(2):
                    dve.wait_ge(osq_done, g * 2 + a + 1)
                    nc.vector.scalar_tensor_tensor(out=osq[:, a, :], in0=qsq[:, :], scalar=EPS * P * P, in1=osq[:, a, :],
                                                   op0=ALU.mult, op1=ALU.add).then_inc(osum_done, 1)
                for a in range(2):
                    dve.wait_ge(rstd_done, g * 2 + a + 1)
                    nc.vector.scalar_tensor_tensor(out=rstd[:, a, :], in0=bank[4 + a][:, :], scalar=nw, in1=rstd[:, a, :],
                                                   op0=ALU.mult, op1=ALU.mult).then_inc(of_made, 1)
                for a in range(2):
                    dve.wait_ge(of_made, g * 2 + a + 1)
                    dve.wait_ge(zsilu_done, g * 2 + a + 1)
                    nc.vector.tensor_tensor(ost[:, bass.ds(g * 2 + a, 1), :].squeeze(1), rstd[:, a, :], sz[:, a, :],
                                            ALU.mult).then_inc(fin_done, 1)

            with dve.Fori(0, GROUPS - 1) as g:
                delta_rule(g, False)
            delta_rule(GROUPS - 1, True)

            for c in range(KD):
                dve.wait_ge(units_used, U_OUT + 13 + c if c < 4 else U_OUT + 4 * (c + 1))
                nc.vector.tensor_tensor(xt[:, c, :], bank[OUT_BANK[c]][:, :], xt[:, c, :], ALU.add).then_inc(x1_done, 1)
                dve.wait_ge(h2_hi_ready, c + 1)
                nc.vector.scalar_tensor_tensor(out=h2_lo[:, c, :], in0=xt[:, c, :], scalar=ffnw[:, c:c + 1],
                                               in1=h2_hi[:, c, :].bitcast(F32), op0=ALU.mult,
                                               op1=ALU.subtract).then_inc(h2_lo_ready, 1)
            dve.wait_ge(rstd2_done, 1)

            def ffn_pair(f0, n0):
                for f in range(2):
                    dve.wait_ge(units_used, n0 + (4 * f + 2))
                    nc.vector.tensor_tensor(tmp[:, f, :], bank[f][:, :], rstd2[:, :], ALU.mult).then_inc(gs_done, 1)
                    dve.wait_ge(units_used, n0 + (4 * f + 4))
                    dve.wait_ge(sg_done, f0 + (f + 1))
                    nc.vector.tensor_tensor(tmp[:, f, :], bank[2 + f][:, :], tmp[:, f, :], ALU.mult).then_inc(prod_done, 1)
                    dve.wait_ge(prod_done, f0 + (f + 1))
                    nc.vector.tensor_tensor(tmp[:, f, :], tmp[:, f, :], rstd2[:, :], ALU.mult).then_inc(prod2_done, 1)
                    dve.wait_ge(act_hi_ready, f0 + (f + 1))
                    at = bass.ds(f0 + f, 1)
                    nc.vector.tensor_tensor(act_lo[:, at, :].squeeze(1), tmp[:, f, :], act_hi[:, at, :].squeeze(1).bitcast(F32),
                                            ALU.subtract).then_inc(act_lo_ready, 1)

            with dve.Fori(0, 5) as i:
                ffn_pair(i * 4, i * 16 + U_FFN)
                ffn_pair(i * 4 + 2, i * 16 + (U_FFN + 8))
            ffn_pair(20, U_FFN + 80)
            for c in range(KD):
                dve.wait_ge(units_used, U_DOWN + 4 * (c + 1))
                nc.vector.tensor_tensor(xt[:, c, :], bank[6 + c % 2][:, :], xt[:, c, :], ALU.add).then_inc(x2_done, 1)
            dve.wait_ge(rstd3_done, 1)
            for t in range(NT):
                nc.vector.tensor_scalar(ytok[:, t, 0:T], ytok[:, t, 0:T], rstd3[:, t:t + 1], None, ALU.mult).then_inc(y_done[t], 1)
            dve.wait_ge(yt_in_bank, KD)
            for t in range(2, NT):
                nc.vector.tensor_scalar(ytok[:, t, T:2 * T], bank[t][:, :], rstd3[:, t:t + 1], None, ALU.mult).then_inc(y_done[t], 1)


INPUTS = ("x", "gdn_w_in", "gdn_conv_w", "gdn_a_log", "gdn_dt_bias", "gdn_norm_w", "gdn_w_out",
          "mix_norm_w", "ffn_norm_w", "ffn_w_gate", "ffn_w_up", "ffn_w_down")


def kernel(**inputs):
    import concourse.bacc as bacc
    from concourse.bass_utils import run_bass_kernel_spmd

    nc = bacc.Bacc("TRN2", target_bir_lowering=False, num_devices=1)
    arrays = {name: np.ascontiguousarray(np.asarray(inputs[name])[0]) for name in INPUTS}
    arrays["final_norm_w"] = np.ascontiguousarray(inputs["final_norm_w"])
    arrays["shape_constants"] = shape_constants()
    args = [nc.dram_tensor(f"in_{name}", a.shape, F32, kind="ExternalInput").ap() for name, a in arrays.items()]
    result = nc.dram_tensor("result", (T, D), F32, kind="ExternalOutput").ap()
    build(nc, *args, result)
    r = run_bass_kernel_spmd(nc, [{f"in_{name}": a for name, a in arrays.items()}], core_ids=[0])
    return r.results[0]["result"].reshape(1, T, D)
```

```python
from contextlib import ExitStack

import numpy as np

import concourse.bass as bass
from concourse import mybir

F32 = mybir.dt.float32
F32R = mybir.dt.float32r
ALU = mybir.AluOpType
ACT = mybir.ActivationFunctionType

P = 128
D = 1024
T = 512
NT = T // P
KD = D // P
HEADS = 16
GROUPS = HEADS // 2
CONV = 4
PADC = CONV - 1
FFN = 2816
KF = FFN // P
EPS = 1e-6
CONV_DIM = 4096
VAL = 2048
KO = VAL // P
LEVELS = (1, 2, 3, 4, 5, 6, 7)
IDENT, INCL, STRICT, PAIR = range(4)
LEVEL0 = 4
NCONST = LEVEL0 + len(LEVELS)
K_G, K_GC, K_NEG_EGC, K_DEC, K_EGL, K_BETA = range(6)
HALF = 4
RING = 4
SLOT_K = 6
UNITS_GROUP = 12
U_OUT = GROUPS * UNITS_GROUP
U_FFN = U_OUT + 4 * KD
U_DOWN = U_FFN + 4 * KF
DOWN_K = (6, 6, 5, 5)

Z_SLICES, QKV_SLICES = 16, 32
FILL = {"y0": 3, "y1": 1}
for _l in LEVELS:
    FILL[f"p{_l}"] = 1
    FILL[f"x{_l}"] = 1
FILL["p1"] = 2
FILL.update({"t": 4, "r": 4, "f": 4})
for _t in range(NT):
    FILL[f"z{_t}"] = 1
    FILL[f"s{_t}"] = 1
FILL.update({"kn": 4, "kk": 0, "end": 48})
FILL_LAST = {"y0": 5, "y1": 1, "p1": 2, "x1": 2, "p2": 2, "x2": 2, "p3": 1, "x3": 1, "p4": 0, "x4": 0, "p5": 0,
             "x5": 0, "p6": 0, "x6": 1, "p7": 2, "x7": 2, "t": 3, "r": 4, "f": 3, "z0": 1, "s0": 1, "z1": 1,
             "s1": 1, "z2": 1, "s2": 1, "z3": 1, "s3": 2, "kn": 3, "end": 21}
ROUNDED = {"p4": ("u0",), "p5": ("u1", "h0", "h1"), "p6": ("h2", "h3"), "p7": ("h4", "u2"), "t": ("h5", "h6", "h7"),
           "r": ("u3", "u4", "h8", "h9"), "z0": ("h10", "h11", "u5"), "z1": ("h12", "u6", "h13"), "z2": ("u7",),
           "kn": ("u8", "u9")}
ROUNDED_LATER = ("u10", "h14", "h15", "u11", "u12", "u13", "u14", "u15")
V_SILU_LEVEL = 5
NLE_SET = "natural_log_exp_and_others"


def shape_constants():
    i = np.arange(P)
    row, col = i[:, None], i[None, :]
    eye = (row == col).astype(np.float32)
    tabs = [eye, (row <= col).astype(np.float32), (row < col).astype(np.float32),
            eye - ((col == row + 1) & (row % 2 == 0)).astype(np.float32)]
    for lv in LEVELS:
        b = 1 << (lv - 1)
        off = (row // (2 * b) == col // (2 * b)) & ((row // b) % 2 == 1) & ((col // b) % 2 == 0)
        tabs.append(eye - off.astype(np.float32))
    return np.ascontiguousarray(np.stack(tabs, 1).astype(np.float32).reshape(P, NCONST * P))


def build(nc, x, w_in, conv_w, a_log, dt_bias, norm_w, w_out, mix_w, ffn_w, w_gate, w_up, w_down,
          fin_w, consts, out):
    with ExitStack() as ctx:
        def sem(name):
            return ctx.enter_context(nc.semaphore(name))

        place = [nc.sbuf_base + (-nc.sbuf_base) % 32]

        def sb(name, shape, dt=F32, at=None):
            size = 4
            for n in shape[1:]:
                size *= n
            where = place[0] if at is None else at
            if at is None:
                place[0] += -(-size // 32) * 32
            return nc.alloc_sbuf_tensor_at(name, shape, dt, offset=where)

        cst = sb("cst", [P, NCONST, P])
        ones = sb("ones", [P, P])
        cw = sb("cw", [P, GROUPS, 4, CONV])
        vcol = sb("vcol", [P, 3 * KD + 1])
        mixw, ffnw, finw, nw = vcol[:, 0:KD], vcol[:, KD:2 * KD], vcol[:, 2 * KD:3 * KD], vcol[:, 3 * KD:]
        biases = sb("biases", [P, 4])
        B_ZERO, B_EPS, B_ONE, B_QEPS = range(4)
        wraw_at = place[0]
        wraw = [sb(f"wraw{s}", [P, KD, 2 * P]) for s in range(4)]
        whi = [sb(f"whi{s}", [P, SLOT_K, P], F32R) for s in range(RING)]
        wlo = [sb(f"wlo{s}", [P, SLOT_K, P], F32R) for s in range(RING)]
        wout_raw = [sb(f"wout_raw{s}", [P, KO, P], at=wraw_at + 8192 * s) for s in range(4)]
        wdown_raw = [sb("wdown_raw0", [P, KF, P], at=wraw_at + 16384),
                     sb("wdown_raw1", [P, KF, P], at=wraw_at)]
        base = place[0]

        h_hi = sb("h_hi", [P, KD, T], F32R)
        h_lo = sb("h_lo", [P, KD, T], F32R)
        work = place[0]
        raw = sb("raw", [P, 4, PADC + T])
        kq = sb("kq", [P, NT, 2, P])
        va_at = place[0]
        va = sb("va", [P, 2, T])
        vn = sb("vn", [P, 2, NT, P], at=va_at)
        sz = sb("sz", [P, 2, T])
        a_at = place[0]
        amat = sb("amat", [P, 2, NT, P])
        osq = sb("osq", [P, 2, T], at=a_at)
        x_at = place[0]
        xmat = sb("xmat", [P, 2, NT, P])
        yfin = sb("yfin", [P, 2, NT, P], at=x_at)
        rstd = sb("rstd", [P, 2, T], at=x_at)
        d_at = place[0]
        yr = sb("yr", [P, 2, NT, 2, P], F32R)
        dmat = sb("dmat", [P, 2, NT, P], at=d_at)
        dcmat = sb("dcmat", [P, 2, NT, P])
        p_at = place[0]
        pmat = sb("pmat", [P, 2, NT, P], F32R)
        fmat = sb("fmat", [P, 2, NT, P], F32R, at=p_at)
        qhat = sb("qhat", [P, 2, NT, P])
        attn = sb("attn", [P, 2, NT, P])
        kdec = sb("kdec", [P, 2, NT, P])
        qk, ktok = attn[:, 1, :, :], kdec[:, 1, :, :]
        qsq = sb("qsq", [P, T])
        ksq = sb("ksq", [P, NT, P], at=x_at)
        ksum = sb("ksum", [P, NT])
        rbuf = sb("rbuf", [P, 2, P])
        zbuf = sb("zbuf", [P, 2, P])
        state = sb("state", [P, 2, P])
        gates = sb("gates", [P, 6, HEADS, NT])
        gg = sb("gg", [P, 6, 2, NT])
        cwg = sb("cwg", [P, 4, CONV])
        gc_parts = sb("gc_parts", [P, P], F32R)
        pick = sb("pick", [P, HEADS * NT], F32R)
        pickg = sb("pickg", [P, 2, NT], F32R)
        s1 = sb("s1", [P, NT])
        rc = sb("rc", [P, NT])
        nk = sb("nk", [P, NT])
        cc = sb("cc", [P, 2, NT])
        cd = sb("cd", [P, 2, NT])
        ost_at = place[0]
        ost = sb("ost", [P, HEADS, T])
        xt_at = place[0]
        xt = sb("xt", [P, KD, T])
        assert place[0] <= nc.sbuf_usable_end, place[0]
        xs = sb("xs", [P, NT, D], at=work)
        xn = sb("xn", [P, NT, D], at=work + 16384)
        ss = sb("ss", [P, NT], at=work + 32768)
        rs = sb("rs", [P, NT], at=work + 32800)
        place0 = place[0]
        place[0] = work + 32832
        ba_raw = sb("ba_raw", [P, KD, P])
        ba_hi = sb("ba_hi", [P, KD, P], F32R)
        ba_lo = sb("ba_lo", [P, KD, P], F32R)
        bat = sb("bat", [P, T])
        vrow = sb("vrow", [3 * KD + 1, P])
        alog = sb("alog", [P, HEADS])
        dtb = sb("dtb", [P, HEADS])
        ealog = sb("ealog", [P, HEADS])
        bt = sb("bt", [P, NT, HEADS])
        yt = sb("yt", [P, NT, HEADS])
        ab = sb("ab", [P, NT, HEADS])
        sp_ = sb("sp_", [P, NT, HEADS])
        gl_gc = sb("gl_gc", [P, HEADS * NT])
        gc_twice = sb("gc_twice", [P, 2, HEADS * NT])
        gc_first = sb("gc_first", [P, P], F32R)
        o_hi = sb("o_hi", [P, KO, T], F32R, at=base)
        o_lo = sb("o_lo", [P, KO, T], F32R, at=ost_at)
        place[0] = base
        act_lo = sb("act_lo", [P, KF, T], F32R)
        h2_at = place[0]
        h2_hi = sb("h2_hi", [P, KD, T], F32R)
        h2_lo = sb("h2_lo", [P, KD, T], F32R)
        sq = sb("sq", [P, 3, T], at=place[0])
        act_hi = sb("act_hi", [P, KF, T], F32R)
        tmp = sb("tmp", [P, 2, T])
        rstd2_at = place[0]
        rstd2 = sb("rstd2", [P, T])
        rstd3 = sb("rstd3", [P, NT])
        x2sum = sb("x2sum", [P, T], at=rstd2_at)[:, :]
        assert place[0] <= xt_at and base + 32768 <= h2_at
        yw = sb("yw", [P, 2, T], at=h2_at)
        ytok = sb("ytok", [P, NT, D], at=h2_at + 16384)

        bank = [ctx.enter_context(nc.psum_tensor(f"bank{i}", [P, T], F32)) for i in range(8)]
        b4 = [b[:, :].rearrange("p (t i) -> p t i", i=P) for b in bank]
        ident = cst[:, IDENT, :]

        def over_tiles(table):
            return cst[:, table, :].unsqueeze(1).to_broadcast([P, NT, P])

        def per_token(col, n=NT):
            return col.unsqueeze(2).to_broadcast([P, n, P])

        x_in = [sem(f"x_in{t}") for t in range(NT)]
        const_in = sem("const_in")
        ident_in = sem("ident_in")
        small_in = sem("small_in")
        vec_in = sem("vec_in")
        ba_in = sem("ba_in")
        w1_in = [sem(f"w1_in{i}") for i in range(3)]
        wo_in = [sem(f"wo_in{i}") for i in range(4)]
        wf_in = [sem(f"wf_in{i}") for i in range(4)]
        wd_in = [sem(f"wd_in{i}") for i in range(2)]
        y_out = sem("y_out")
        hi_ready = sem("hi_ready")
        lo_ready = sem("lo_ready")
        ba_hi_ready = sem("ba_hi_ready")
        ba_ready = sem("ba_ready")
        units_used = sem("units_used")
        slot_free = sem("slot_free")
        ones_set = sem("ones_set")
        bias_set = sem("bias_set")
        pad_set = sem("pad_set")
        ss_ready = sem("ss_ready")
        ln_ready = sem("ln_ready")
        rs_ready = sem("rs_ready")
        xn_ready = sem("xn_ready")
        vec_in_bank = sem("vec_in_bank")
        vec_done = sem("vec_done")
        xt_in_bank = sem("xt_in_bank")
        xt_copied = sem("xt_copied")
        h_in_bank = sem("h_in_bank")
        h_hi_ready = sem("h_hi_ready")
        h_lo_ready = sem("h_lo_ready")
        ba_in_bank = sem("ba_in_bank")
        bat_copied = sem("bat_copied")
        ba_turned = sem("ba_turned")
        gate_act = sem("gate_act")
        gate_dve = sem("gate_dve")
        sums_in_bank = sem("sums_in_bank")
        gc_twice_made = sem("gc_twice_made")
        gc_turned = sem("gc_turned")
        gc_first_made = sem("gc_first_made")
        gc_parts_made = sem("gc_parts_made")
        pick_made = sem("pick_made")
        bc_done = sem("bc_done")
        kk_done = sem("kk_done")
        kt_done = sem("kt_done")
        vt_done = sem("vt_done")
        p_done = sem("p_done")
        yr_done = sem("yr_done")
        xt_done = sem("xt_done")
        res_done = sem("res_done")
        yf_done = sem("yf_done")
        ks_done = sem("ks_done")
        z_done = sem("z_done")
        o_done = sem("o_done")
        sn_done = sem("sn_done")
        oss_done = sem("oss_done")
        evac_done = sem("evac_done")
        egrow_done = sem("egrow_done")
        dexp_done = sem("dexp_done")
        silu_done = sem("silu_done")
        vsilu_done = sem("vsilu_done")
        zsilu_done = sem("zsilu_done")
        sq_done = sem("sq_done")
        qk_copied = sem("qk_copied")
        ktok_copied = sem("ktok_copied")
        ksq_done = sem("ksq_done")
        nkln_done = sem("nkln_done")
        nk_done = sem("nk_done")
        ar_done = sem("ar_done")
        x_copied = sem("x_copied")
        z_copied = sem("z_copied")
        yr_copied = sem("yr_copied")
        osq_done = sem("osq_done")
        oln_done = sem("oln_done")
        rstd_done = sem("rstd_done")
        gg_done = sem("gg_done")
        cwg_done = sem("cwg_done")
        arg_done = sem("arg_done")
        conv_step = sem("conv_step")
        conv_done = sem("conv_done")
        vconv_step = sem("vconv_step")
        vconv_done = sem("vconv_done")
        s1_done = sem("s1_done")
        c_chain = sem("c_chain")
        qhat_done = sem("qhat_done")
        kdec_done = sem("kdec_done")
        dc_done = sem("dc_done")
        dg_done = sem("dg_done")
        attn_done = sem("attn_done")
        a_chain = sem("a_chain")
        a_done = sem("a_done")
        y1_done = sem("y1_done")
        vn_done = sem("vn_done")
        pm_done = sem("pm_done")
        r_done = sem("r_done")
        f_done = sem("f_done")
        yf_added = sem("yf_added")
        s_done = sem("s_done")
        osum_done = sem("osum_done")
        of_made = sem("of_made")
        fin_done = sem("fin_done")
        o_hi_ready = sem("o_hi_ready")
        o_lo_ready = sem("o_lo_ready")
        x1_done = sem("x1_done")
        x1sq_done = sem("x1sq_done")
        x1add_done = sem("x1add_done")
        x2add_done = sem("x2add_done")
        x1ss_done = sem("x1ss_done")
        x1ln_done = sem("x1ln_done")
        rstd2_done = sem("rstd2_done")
        h2_hi_ready = sem("h2_hi_ready")
        h2_lo_ready = sem("h2_lo_ready")
        gs_done = sem("gs_done")
        sg_done = sem("sg_done")
        prod_done = sem("prod_done")
        prod2_done = sem("prod2_done")
        act_hi_ready = sem("act_hi_ready")
        act_lo_ready = sem("act_lo_ready")
        x2_done = sem("x2_done")
        x2sq_done = sem("x2sq_done")
        yw_done = sem("yw_done")
        x2ss_done = sem("x2ss_done")
        x2ln_done = sem("x2ln_done")
        rstd3_done = sem("rstd3_done")
        yt_in_bank = sem("yt_in_bank")
        yt_copied = sem("yt_copied")
        y_done = [sem(f"y_done{t}") for t in range(NT)]

        win = w_in.rearrange("(k p) n -> p k n", p=P)
        wov = w_out.rearrange("(k p) n -> p k n", p=P)
        wgv = w_gate.rearrange("(k p) n -> p k n", p=P)
        wuv = w_up.rearrange("(k p) n -> p k n", p=P)
        wdv = w_down.rearrange("(k p) n -> p k n", p=P)
        cwv = conv_w.rearrange("(n p) j -> p n j", p=P)
        nl = len(LEVELS)

        OUT_BANK = (6, 7, 0, 1, 6, 7, 6, 7)

        def out_source(p):
            if p < 12:
                tile, q = 2 * (p // 6) + p % 2, p % 6 // 2
            elif p < 16:
                tile, q = p - 12, 3
            else:
                tile, q = p // 4, p % 4
            return tile, wout_raw[tile % 4][:, HALF * q:HALF * q + HALF, :], 16 * (tile // 4 + 1)

        def slices_before(fill, step):
            n = 0
            for name in fill:
                n += fill[name]
                if name == step:
                    break
            return n

        block = ctx.enter_context(nc.Block())

        @block.sync
        def _(sp):
            for t in range(NT):
                sp.dma_start(xs[:, t, :], x[t * P:(t + 1) * P, :]).then_inc(x_in[t], 16)
            sp.dma_start(ident, consts[:, IDENT * P:(IDENT + 1) * P]).then_inc(ident_in, 16)
            for n, vec in enumerate((mix_w, ffn_w, fin_w)):
                sp.dma_start(vrow[n * KD:(n + 1) * KD, :], vec.rearrange("(k p) -> k p", p=P)).then_inc(vec_in, 16)
            sp.dma_start(vrow[3 * KD:3 * KD + 1, :], norm_w.unsqueeze(0)).then_inc(vec_in, 16)
            sp.dma_start(ba_raw[:, :, :], win[:, :, CONV_DIM + VAL + 32 - P:CONV_DIM + VAL + 32]).then_inc(ba_in, 16)

            def load_group(g, reuse):
                c = g * P
                if reuse:
                    sp.wait_ge(lo_ready, g * UNITS_GROUP - 8)
                sp.dma_start(wraw[0][:, :, 0:P], win[:, :, bass.ds(c, P)]).then_inc(w1_in[0], 16)
                sp.dma_start(wraw[0][:, :, P:2 * P], win[:, :, bass.ds(c + D, P)]).then_inc(w1_in[0], 16)
                if reuse:
                    sp.wait_ge(lo_ready, g * UNITS_GROUP - 4)
                sp.dma_start(wraw[1][:, :, :], win[:, :, bass.ds(c * 2 + 2 * D, 2 * P)]).then_inc(w1_in[1], 16)
                if reuse:
                    sp.wait_ge(lo_ready, g * UNITS_GROUP)
                sp.dma_start(wraw[2][:, :, :], win[:, :, bass.ds(c * 2 + CONV_DIM, 2 * P)]).then_inc(w1_in[2], 16)

            load_group(0, False)
            sp.dma_start(alog[:, :], a_log.unsqueeze(0).to_broadcast([P, HEADS])).then_inc(small_in, 16)
            sp.dma_start(dtb[:, :], dt_bias.unsqueeze(0).to_broadcast([P, HEADS])).then_inc(small_in, 16)
            for u, first in enumerate((0, KD)):
                sp.dma_start(cw[:, :, u, :], cwv[:, first:first + KD, :]).then_inc(small_in, 16)
            for u in range(2):
                sp.dma_start(cw[:, :, 2 + u, :],
                              cwv[:, 2 * KD:4 * KD, :].rearrange("p (g u) j -> p g u j", u=2)[:, :, u, :]
                              ).then_inc(small_in, 16)
            sp.dma_start(cst[:, 1:, :].rearrange("p a b -> p (a b)"), consts[:, P:]).then_inc(const_in, 16)
            with sp.Fori(1, GROUPS) as g:
                load_group(g, True)
            for c in range(4):
                if c < 3:
                    sp.wait_ge(lo_ready, U_OUT - UNITS_GROUP + 4 * (c + 1))
                sp.dma_start(wout_raw[c][:, :, :], wov[:, :, c * P:(c + 1) * P]).then_inc(wo_in[c], 16)
            for c in range(4, KD):
                sp.wait_ge(lo_ready, U_OUT + 12 + (c - 3))
                sp.dma_start(wout_raw[c - 4][:, :, :], wov[:, :, c * P:(c + 1) * P]).then_inc(wo_in[c - 4], 16)

            def load_pair(j, half, gate_free, up_free):
                sp.wait_ge(lo_ready, gate_free)
                sp.dma_start(wraw[2 * half][:, :, :], wgv[:, :, bass.ds(j * 2 * P, 2 * P)]).then_inc(wf_in[2 * half], 16)
                sp.wait_ge(lo_ready, up_free)
                sp.dma_start(wraw[2 * half + 1][:, :, :], wuv[:, :, bass.ds(j * 2 * P, 2 * P)]).then_inc(wf_in[2 * half + 1], 16)

            load_pair(0, 0, U_OUT + 20, U_OUT + 24)
            load_pair(1, 1, U_OUT + 28, U_OUT + 32)
            with sp.Fori(1, 5) as i:
                load_pair(i * 2, 0, i * 16 + (U_FFN - 16 + 6), i * 16 + (U_FFN - 16 + 8))
                load_pair(i * 2 + 1, 1, i * 16 + (U_FFN - 8 + 6), i * 16 + (U_FFN - 8 + 8))
            load_pair(10, 0, U_FFN + 64 + 6, U_FFN + 64 + 8)
            sp.wait_ge(lo_ready, U_FFN + 80)
            sp.dma_start(wdown_raw[0][:, :, :], wdv[:, :, 0:P]).then_inc(wd_in[0], 16)
            sp.wait_ge(lo_ready, U_DOWN)
            sp.dma_start(wdown_raw[1][:, :, :], wdv[:, :, P:2 * P]).then_inc(wd_in[1], 16)
            with sp.Fori(1, KD // 2) as i:
                for s in range(2):
                    sp.wait_ge(lo_ready, i * 8 + (U_DOWN - 8 + 4 * (s + 1)))
                    sp.dma_start(wdown_raw[s][:, :, :], wdv[:, :, bass.ds(i * 2 * P + s * P, P)]).then_inc(wd_in[s], 16)
            for t in range(NT):
                sp.wait_ge(y_done[t], 2)
                sp.dma_start(out[t * P:(t + 1) * P, :], ytok[:, t, :]).then_inc(y_out, 16)
            sp.wait_ge(y_out, 16 * NT)

        @block.gpsimd
        def _(pool):
            nc.gpsimd.memset(ones[:, :], 1.0).then_inc(ones_set, 1)
            for col, value in ((B_ZERO, 0.0), (B_EPS, EPS), (B_ONE, 1.0), (B_QEPS, EPS * EPS * P)):
                nc.gpsimd.memset(biases[:, col:col + 1], value).then_inc(bias_set, 1)
            pool.wait_ge(ba_hi_ready, 1)
            nc.gpsimd.tensor_tensor(ba_lo[:, :, :], ba_raw[:, :, :], ba_hi[:, :, :].bitcast(F32),
                                    ALU.subtract).then_inc(ba_ready, 1)

            def lo(n, slot, src):
                pool.wait_ge(hi_ready, n + 1)
                nc.gpsimd.tensor_tensor(wlo[slot][:, 0:src.shape[1], :], src, whi[slot][:, 0:src.shape[1], :].bitcast(F32),
                                        ALU.subtract).then_inc(lo_ready, 1)

            def group(g, first):
                for u in range(6):
                    if u == 0:
                        pool.wait_ge(w1_in[0], g * 32 + 32)
                    elif u % 2 == 0:
                        pool.wait_ge(w1_in[u // 2], g * 16 + 16)
                    for hf in range(2):
                        m = 2 * u + hf
                        n = g * UNITS_GROUP + m
                        src = wraw[u // 2][:, HALF * hf:HALF * hf + HALF, (u % 2) * P:(u % 2 + 1) * P]
                        if not (first and m < RING):
                            pool.wait_ge(units_used, n - (RING - 1))
                        if not first:
                            pool.sem_inc(slot_free, 1)
                        nc.gpsimd.tensor_copy(whi[m % RING][:, 0:HALF, :], src).then_inc(hi_ready, 1)
                        lo(n, m % RING, src)

            group(0, True)
            with pool.Fori(1, GROUPS) as g:
                group(g, False)

            def o_lo_of(k):
                pool.wait_ge(o_hi_ready, k + 1)
                nc.gpsimd.tensor_tensor(o_lo[:, k, :], ost[:, k, :], o_hi[:, k, :].bitcast(F32),
                                        ALU.subtract).then_inc(o_lo_ready, 1)

            for name in sum(ROUNDED.values(), ()) + ROUNDED_LATER:
                if name[0] == "u":
                    lo(U_OUT + int(name[1:]), int(name[1:]) % RING, out_source(int(name[1:]))[1])
                else:
                    o_lo_of(int(name[1:]))
            for p in range(16, 4 * KD):
                lo(U_OUT + p, p % RING, out_source(p)[1])

            def pair(n0, half):
                for m in range(8):
                    up, f, hf = (m // 2) % 2, m // 4, m % 2
                    lo(n0 + m, m % RING, wraw[2 * half + up][:, HALF * hf:HALF * hf + HALF, f * P:(f + 1) * P])

            with pool.Fori(0, 5) as i:
                pair(i * 16 + U_FFN, 0)
                pair(i * 16 + (U_FFN + 8), 1)
            pair(U_FFN + 80, 0)
            with pool.Fori(0, KD // 2) as i:
                for s in range(2):
                    for q in range(4):
                        k = sum(DOWN_K[:q])
                        lo(i * 8 + (U_DOWN + 4 * s + q), q, wdown_raw[s][:, k:k + DOWN_K[q], :])

        @block.tensor
        def _(pe):
            pe.wait_ge(ident_in, 16)
            pe.wait_ge(vec_in, 64)
            nv = 3 * KD + 1
            nc.tensor.transpose(bank[7][:, 0:nv], vrow[:, :], cst[0:nv, IDENT, 0:nv]).then_inc(vec_in_bank, 1)
            pe.wait_ge(xn_ready, NT)
            for k in range(KD):
                if k >= 4:
                    pe.wait_ge(h_lo_ready, k - 3)
                for t in range(NT):
                    mm = nc.tensor.transpose(b4[k % 4][:, t, :], xn[:, t, k * P:(k + 1) * P], ident)
                mm.then_inc(h_in_bank, 1)
            pe.wait_ge(ba_ready, 1)
            pe.wait_ge(vec_done, 1)
            for k in range(KD):
                pe.wait_ge(h_lo_ready, k + 1)
                for n, (w, r) in enumerate(((ba_lo, h_hi), (ba_hi, h_lo), (ba_hi, h_hi))):
                    mm = nc.tensor.matmul(bank[7][:, :], w[:, k, :], r[:, k, :],
                                          start=(k == 0 and n == 0), stop=(k == KD - 1 and n == 2))
            mm.then_inc(ba_in_bank, 1)

            def yr_bank(a, t):
                return bank[2 + 2 * a + t // 2][:, :].rearrange("p (t k i) -> p t k i", k=2, i=P)[:, t % 2, :, :]

            def unit(dst, slot, kk, rhs_hi, rhs_lo, k0, first, last):
                for k in range(kk):
                    for n, (w, r) in enumerate(((wlo, rhs_hi), (whi, rhs_lo), (whi, rhs_hi))):
                        mm = nc.tensor.matmul(dst, w[slot][:, k, :], r[:, k0 + k, :],
                                              start=(first and k == 0 and n == 0),
                                              stop=(last and k == kk - 1 and n == 2))
                mm.then_inc(units_used, 1)

            def project(g, n, start=False):
                u, k, m = n // KD, n % KD, n // HALF
                if k == 0:
                    if u < 2 and not start:
                        pe.wait_ge(zsilu_done, g * 2 - (1 - u))
                    elif u == 1:
                        pe.wait_ge(bat_copied, 1)
                    elif u >= 2:
                        pe.wait_ge(evac_done, g * 4 + (u - 1))
                if k % HALF == 0:
                    pe.wait_ge(lo_ready, g * UNITS_GROUP + (m + 1))
                for j, (w, r) in enumerate(((wlo, h_hi), (whi, h_lo), (whi, h_hi))):
                    mm = nc.tensor.matmul(bank[6 + u % 2][:, :], w[m % RING][:, k % HALF, :], r[:, k, :],
                                          start=(k == 0 and j == 0), stop=(k == KD - 1 and j == 2))
                if k % HALF == HALF - 1:
                    mm.then_inc(units_used, 1)

            def out_slice(m):
                p = m // HALF
                tile, q = 2 * (p // 6) + p % 2, p % 6 // 2
                k = HALF * q + m % HALF
                if m % HALF == 0:
                    pe.wait_ge(lo_ready, U_OUT + p + 1)
                if tile == 0:
                    pe.wait_ge(o_lo_ready, k + 1)
                for j, (w, r) in enumerate(((wlo, o_hi), (whi, o_lo), (whi, o_hi))):
                    mm = nc.tensor.matmul(bank[OUT_BANK[tile]][:, :], w[p % RING][:, m % HALF, :], r[:, k, :],
                                          start=(k == 0 and j == 0), stop=False)
                if m % HALF == HALF - 1:
                    mm.then_inc(units_used, 1)

            for n in range(KD):
                project(0, n, True)
            pe.wait_ge(bat_copied, 1)
            for t in range(NT):
                mm = nc.tensor.transpose(b4[4][:, t, :], bat[:, t * P:(t + 1) * P], ident)
            mm.then_inc(ba_turned, 1)
            for k in range(KD):
                pe.wait_ge(x_in[k % NT], 16)
                if k >= 4:
                    pe.wait_ge(xt_copied, k - 3)
                for t in range(NT):
                    mm = nc.tensor.transpose(b4[k % 4][:, t, :], xs[:, t, k * P:(k + 1) * P], ident)
                mm.then_inc(xt_in_bank, 1)
                if k >= 2:
                    project(0, KD + k - 2, True)
            pe.wait_ge(ones_set, 1)
            pe.wait_ge(const_in, 16)
            pe.wait_ge(gate_dve, 6)
            gall = gates[:, K_G, :, :].rearrange("p h t -> p (h t)")
            nc.tensor.matmul(bank[5][:, 0:HEADS * NT], cst[:, INCL, :], gall, start=True, stop=True)
            nc.tensor.matmul(bank[5][:, HEADS * NT:2 * HEADS * NT], ones[:, :], gall,
                             start=True, stop=True).then_inc(sums_in_bank, 1)

            def gc_rows(g):
                pe.wait_ge(gg_done, g + 1)
                for a in range(2):
                    for t in range(NT):
                        mm = nc.tensor.matmul(b4[a][:, t, :], pickg[:, a, t:t + 1].to_broadcast([P, P]),
                                              gc_parts[:, :], start=True, stop=True)
                    mm.then_inc(bc_done, 1)

            def turn_keys(g):
                pe.wait_ge(silu_done, g * 2 + 1)
                for t in range(NT):
                    mm = nc.tensor.transpose(b4[3][:, t, :], kq[:, t, 0, :], ident)
                mm.then_inc(kt_done, 1)

            def key_products(g):
                pe.wait_ge(silu_done, g * 2 + 2)
                pe.wait_ge(egrow_done, g * 2 + 2)
                for t in range(NT):
                    mm = nc.tensor.matmul(bank[t // 2][:, (t % 2) * 256:(t % 2) * 256 + 256],
                                          kq[:, t, 0, :], kq[:, t, :, :].rearrange("p a i -> p (a i)"),
                                          start=True, stop=True)
                mm.then_inc(kk_done, 1)

            for n in range(KD + 6, 2 * KD):
                project(0, n, True)
            pe.wait_ge(gc_twice_made, 2)
            nc.tensor.transpose(bank[5][:, P:2 * P], gc_twice[:, :, :].rearrange("p k n -> p (k n)"),
                                ident).then_inc(gc_turned, 1)
            for n in range(2 * KD, 2 * KD + 4):
                project(0, n)
            gc_rows(0)
            for n in range(2 * KD + 4, QKV_SLICES):
                project(0, n)
            turn_keys(0)
            key_products(0)

            def delta_rule(g, last):
                plan = FILL_LAST if last else FILL
                issued = [0]

                def fill(step):
                    for _ in range(plan[step]):
                        n = issued[0]
                        if n < Z_SLICES:
                            project(g, QKV_SLICES + n)
                        elif last and n < Z_SLICES + 48:
                            out_slice(n - Z_SLICES)
                        elif n < Z_SLICES + QKV_SLICES:
                            project(g + 1, n - Z_SLICES)
                        issued[0] += 1

                for a in range(2):
                    fill(f"y{a}")
                    pe.wait_ge(qk_copied, g * 2 + 2)
                    pe.wait_ge(a_done, g * 2 + a + 1)
                    for t in range(NT):
                        mm = nc.tensor.transpose(b4[a][:, t, :], amat[:, a, t, :], ident)
                    mm.then_inc(p_done, 1)
                for i, lv in enumerate(LEVELS):
                    for a in range(2):
                        fill(f"{'px'[a]}{lv}")
                        pe.wait_ge(pm_done, g * (2 * nl) + 2 * i + a + 1)
                        if i == 0:
                            pe.wait_ge(ar_done, g * 2 + a + 1)
                        else:
                            pe.wait_ge(yr_copied, g * (2 * nl) + 2 * (i - 1) + a + 1)
                        if i == 1:
                            pe.wait_ge(y1_done, g * 2 + a + 1)
                        if i < nl - 1:
                            for t in range(NT):
                                mm = nc.tensor.matmul(b4[a][:, t, :], yr[:, a, t, 1, :], pmat[:, a, t, :],
                                                      start=True, stop=True)
                            mm.then_inc(p_done, 1)
                        lo_half, hi_half = (1 if i == 0 else 0), (1 if i == nl - 1 else 2)
                        for t in range(NT):
                            dst = yr_bank(a, t)[:, lo_half:hi_half, :].rearrange("p k i -> p (k i)")
                            src = yr[:, a, t, lo_half:hi_half, :].rearrange("p k i -> p (k i)")
                            mm = nc.tensor.matmul(dst, pmat[:, a, t, :], src, start=True, stop=True)
                        mm.then_inc(yr_done, 1)
                for a in range(2):
                    if a == 0:
                        fill("t")
                    pe.wait_ge(yr_copied, g * (2 * nl) + 2 * (nl - 1) + a + 1)
                    for t in range(NT):
                        mm = nc.tensor.transpose(b4[a][:, t, :], yr[:, a, t, 0, :].bitcast(F32), ident)
                    mm.then_inc(xt_done, 1)
                fill("r")
                for a in range(2):
                    pe.wait_ge(x_copied, g * 2 + a + 1)
                    for t in range(NT):
                        mm = nc.tensor.matmul(b4[a][:, t, :], amat[:, a, t, :], xmat[:, a, t, :],
                                              start=True, stop=True)
                    mm.then_inc(res_done, 1)
                for a in range(2):
                    pe.wait_ge(vsilu_done, g * 2 + a + 1)
                    for t in range(NT):
                        mm = nc.tensor.transpose(b4[2 + a][:, t, :], va[:, a, t * P:(t + 1) * P], ident)
                    mm.then_inc(vt_done, 1)
                fill("f")
                for a in range(2):
                    pe.wait_ge(f_done, g * 2 + a + 1)
                    for t in range(NT):
                        mm = nc.tensor.matmul(b4[4 + a][:, t, :], fmat[:, a, t, :], yr[:, a, t, 0, :],
                                              start=True, stop=True)
                    mm.then_inc(yf_done, 1)
                for t in range(NT):
                    if t > 0:
                        pe.wait_ge(s_done, g * 6 + 2 * t)
                        nc.tensor.matmul(bank[0][:, 0:2 * P], kq[:, t, 0, :],
                                         state[:, :, :].rearrange("p a i -> p (a i)"),
                                         start=True, stop=True).then_inc(ks_done, 1)
                    fill(f"z{t}")
                    for a in range(2):
                        if t == 0:
                            pe.wait_ge(yf_added, g * 2 + a + 1)
                            pe.wait_ge(vn_done, g * 2 + a + 1)
                            rhs = vn[:, a, 0, :]
                        else:
                            pe.wait_ge(r_done, g * 6 + 2 * (t - 1) + a + 1)
                            rhs = rbuf[:, a, :]
                        mm = nc.tensor.matmul(bank[1][:, a * P:(a + 1) * P], yfin[:, a, t, :], rhs,
                                              start=True, stop=True)
                    mm.then_inc(z_done, 1)
                    if t > 0:
                        for a in range(2):
                            nc.tensor.matmul(b4[4 + a][:, t, :], state[:, a, :], qhat[:, a, t, :],
                                             start=True, stop=False)
                    if t == 0:
                        fill("s0")
                    pe.wait_ge(z_copied, g * NT + t + 1)
                    if t < NT - 1:
                        if t == 0:
                            pe.wait_ge(vn_done, g * 2 + 2)
                            pe.wait_ge(kdec_done, g * 2 + 2)
                        for a in range(2):
                            mm = nc.tensor.matmul(bank[2][:, a * P:(a + 1) * P], kdec[:, a, t, :], zbuf[:, a, :],
                                                  start=True, stop=True)
                        mm.then_inc(sn_done, 1)
                    if t == 0:
                        pe.wait_ge(qhat_done, g * 2 + 2)
                        pe.wait_ge(attn_done, g * 2 + 2)
                    for a in range(2):
                        mm = nc.tensor.matmul(b4[4 + a][:, t, :], zbuf[:, a, :], attn[:, a, t, :],
                                              start=(t == 0), stop=True)
                    if t == NT - 1:
                        mm.then_inc(o_done, 1)
                    if t > 0:
                        fill(f"s{t}")
                if not last:
                    turn_keys(g + 1)
                    gc_rows(g + 1)
                fill("kn")
                for a in range(2):
                    if a == 1 and not last:
                        pe.wait_ge(ktok_copied, g + 2)
                        pe.wait_ge(ksq_done, g * 4 + 8)
                    pe.wait_ge(osum_done, g * 2 + a + 1)
                    nc.tensor.matmul(bank[2 + a][:, :], ones[:, :], osq[:, a, :],
                                     start=True, stop=True).then_inc(oss_done, 1)
                if not last:
                    fill("kk")
                    key_products(g + 1)
                fill("end")

            with pe.Fori(0, GROUPS - 1) as g:
                delta_rule(g, False)
            delta_rule(GROUPS - 1, True)

            pe.wait_ge(fin_done, HEADS)
            pe.wait_ge(o_lo_ready, KO)
            for tile in range(4):
                pe.wait_ge(lo_ready, U_OUT + 12 + tile + 1)
                unit(bank[OUT_BANK[tile]][:, :], tile, HALF, o_hi, o_lo, 3 * HALF, False, True)
            for c in range(4, KD):
                pe.wait_ge(x1_done, (1, 2, 5, 6)[c - 4])
                for q in range(4):
                    pe.wait_ge(lo_ready, U_OUT + 4 * c + q + 1)
                    unit(bank[OUT_BANK[c]][:, :], q, HALF, o_hi, o_lo, HALF * q, q == 0, q == 3)

            def ffn_tile(n0, up, f, par, free, first_pass=False):
                if free:
                    pe.wait_ge(prod_done if up else gs_done, f - 1)
                for hf in range(2):
                    pe.wait_ge(lo_ready, n0 + (hf + 1))
                    if first_pass and hf == 1:
                        pe.wait_ge(h2_lo_ready, KD)
                    elif first_pass:
                        pe.wait_ge(h2_lo_ready, KD // 2)
                    unit(bank[2 * up + par][:, :], 2 * up + hf, HALF, h2_hi, h2_lo, HALF * hf, hf == 0, hf == 1)

            def ffn_pair(n0, f0, free):
                for f in range(2):
                    for up in range(2):
                        ffn_tile(n0 + (4 * f + 2 * up), up, f0 + f, f, free)

            ffn_tile(U_FFN, 0, 0, 0, False, True)
            pe.wait_ge(x1add_done, KD - 2)
            nc.tensor.matmul(bank[5][:, :], ones[:, :], sq[:, 2, :], start=True, stop=False)
            pe.wait_ge(x1sq_done, KD)
            nc.tensor.matmul(bank[5][:, :], ones[:, :], sq[:, 1, :], start=False, stop=True).then_inc(x1ss_done, 1)
            ffn_tile(U_FFN + 2, 1, 0, 0, False)
            ffn_tile(U_FFN + 4, 0, 1, 1, False)
            ffn_tile(U_FFN + 6, 1, 1, 1, False)
            ffn_pair(U_FFN + 8, 2, True)
            with pe.Fori(1, 5) as i:
                ffn_pair(i * 16 + U_FFN, i * 4, True)
                ffn_pair(i * 16 + (U_FFN + 8), i * 4 + 2, True)
            ffn_pair(U_FFN + 80, 20, True)

            pe.wait_ge(rstd2_done, 1)
            nc.tensor.matmul(bank[5][:, 0:NT], ones[:, :], biases[:, B_ZERO:B_ZERO + 1].to_broadcast([P, NT]),
                             start=True, stop=False, skip_group_check=True)

            def down_tile(n0, c, s, free, first=False):
                if free:
                    pe.wait_ge(x2_done, c - 1)
                k0 = 0
                for q in range(4):
                    pe.wait_ge(lo_ready, n0 + (q + 1))
                    if first:
                        pe.wait_ge(act_lo_ready, k0 + DOWN_K[q])
                    unit(bank[6 + s][:, :], q, DOWN_K[q], act_hi, act_lo, k0, q == 0, q == 3)
                    k0 += DOWN_K[q]

            def finish_tile(c, s):
                if c >= KD - 2:
                    pe.wait_ge(*((x2add_done, KD - 2) if c == KD - 2 else (x2sq_done, KD)))
                    squares = x2sum if c == KD - 2 else tmp[:, s, :]
                    for t in range(NT):
                        mm = nc.tensor.matmul(bank[5][:, t:t + 1], squares[:, t * P:(t + 1) * P], ones[:, 0:1],
                                              start=False, stop=False, skip_group_check=True)
                    mm.then_inc(x2ss_done, 1)
                pe.wait_ge(yw_done, c + 1)
                for t in range(NT):
                    dst = bank[t][:, (c % 4) * P:(c % 4 + 1) * P]
                    mm = nc.tensor.transpose(dst, yw[:, s, t * P:(t + 1) * P], ident)
                mm.then_inc(yt_in_bank, 1)

            for c in range(KD):
                down_tile(U_DOWN + 4 * c, c, c % 2, c >= 2, c == 0)
                if c == 1:
                    pe.wait_ge(prod_done, KF)
                if c == 5:
                    pe.wait_ge(yt_copied, NT)
                if c >= 1:
                    finish_tile(c - 1, (c - 1) % 2)
            finish_tile(KD - 1, 1)

        @block.scalar
        def _(act):
            act.preload_act_table_set(NLE_SET)
            for t in range(NT):
                act.wait_ge(x_in[t], 16)
                nc.scalar.activation(xn[:, t, :], xs[:, t, :], ACT.Square, accum_out=ss[:, t:t + 1]).then_inc(ss_ready, 1)
            act.wait_ge(bias_set, 4)
            act.wait_ge(ss_ready, NT)
            nc.scalar.activation(rs[:, :], ss[:, :], ACT.Ln, bias=biases[:, B_EPS:B_EPS + 1], scale=1.0 / D).then_inc(ln_ready, 1)
            act.wait_ge(ln_ready, 1)
            nc.scalar.activation(rs[:, :], rs[:, :], ACT.Exp, scale=-0.5).then_inc(rs_ready, 1)
            act.wait_ge(vec_in_bank, 1)
            nc.scalar.copy(vcol[:, :], bank[7][:, 0:3 * KD + 1]).then_inc(vec_done, 1)
            act.wait_ge(ba_in, 16)
            nc.scalar.copy(ba_hi[:, :, :], ba_raw[:, :, :]).then_inc(ba_hi_ready, 1)
            act.wait_ge(vec_done, 1)
            for k in range(KD):
                act.wait_ge(h_in_bank, k + 1)
                nc.scalar.activation(h_hi[:, k, :], bank[k % 4][:, :], ACT.Copy, scale=mixw[:, k:k + 1]).then_inc(h_hi_ready, 1)
            act.wait_ge(small_in, 96)
            nc.scalar.activation(ealog[:, :], alog[:, :], ACT.Exp).then_inc(gate_act, 1)
            act.wait_ge(ba_in_bank, 1)
            nc.scalar.copy(bat[:, :], bank[7][:, :]).then_inc(bat_copied, 1)
            act.wait_ge(ba_turned, 1)
            nc.scalar.activation(bt[:, :, :], b4[4][:, :, P - 32:P - 16], ACT.Exp, scale=-1.0).then_inc(gate_act, 1)
            act.wait_ge(gate_dve, 2)
            nc.scalar.activation(ab[:, :, :], ab[:, :, :], ACT.Exp, scale=-1.0).then_inc(gate_act, 1)
            act.wait_ge(gate_act, 3)
            nc.scalar.activation(ab[:, :, :], ab[:, :, :], ACT.Ln, bias=biases[:, B_ONE:B_ONE + 1]).then_inc(gate_act, 1)
            for k in range(KD):
                act.wait_ge(xt_in_bank, k + 1)
                nc.scalar.copy(xt[:, k, :], bank[k % 4][:, :]).then_inc(xt_copied, 1)

            def evac(g, u):
                act.wait_ge(units_used, g * UNITS_GROUP + 2 * (u + 1))
                nc.scalar.copy(raw[:, u, PADC:PADC + T], bank[6 + u % 2][:, :]).then_inc(evac_done, 1)

            act.wait_ge(sums_in_bank, 1)
            flat = [gates[:, k, :, :].rearrange("p h t -> p (h t)") for k in range(6)]
            nc.scalar.activation(flat[K_NEG_EGC], bank[5][:, 0:HEADS * NT], ACT.Exp).then_inc(gate_act, 1)
            nc.scalar.activation(flat[K_EGL], bank[5][:, HEADS * NT:2 * HEADS * NT], ACT.Exp).then_inc(gate_act, 1)
            act.wait_ge(gate_dve, 9)
            nc.scalar.activation(flat[K_DEC], gl_gc[:, :], ACT.Exp).then_inc(gate_act, 1)
            act.wait_ge(gc_turned, 1)
            half = HEADS * NT
            nc.scalar.copy(gc_parts[0:half, :], bank[5][0:half, P:2 * P]).then_inc(gc_first_made, 1)
            nc.scalar.copy(gc_first[half:P, :], bank[5][half:P, P:2 * P]).then_inc(gc_first_made, 1)
            act.wait_ge(pad_set, 1)
            evac(0, 0)
            evac(0, 1)

            def silu_kq(g):
                for n in range(2):
                    act.wait_ge(conv_done, g * 2 + n + 1)
                    nc.scalar.activation(kq[:, :, n, :], dcmat[:, n, :, :], ACT.Silu).then_inc(silu_done, 1)

            def take_keys(g):
                act.wait_ge(kt_done, g + 1)
                nc.scalar.copy(ktok[:, :, :], b4[3][:, :, :]).then_inc(ktok_copied, 1)
                for t in range(NT):
                    nc.scalar.activation(ksq[:, t, :], b4[3][:, t, :], ACT.Square, accum_out=ksum[:, t:t + 1]).then_inc(ksq_done, 1)

            def square_q(g):
                act.wait_ge(silu_done, g * 2 + 2)
                nc.scalar.activation(qsq[:, :].rearrange("p (t i) -> p t i", i=P), kq[:, :, 1, :],
                                     ACT.Square).then_inc(sq_done, 1)

            def decay(g):
                for a in range(2):
                    act.wait_ge(arg_done, g * 2 + a + 1)
                    nc.scalar.activation(qhat[:, a, :, :], b4[a][:, :, :], ACT.Exp).then_inc(egrow_done, 1)
                for a in range(2):
                    nc.scalar.activation(dmat[:, a, :, :], dmat[:, a, :, :], ACT.Exp).then_inc(dexp_done, 1)

            def key_length(g):
                act.wait_ge(s1_done, g + 1)
                nc.scalar.activation(nk[:, :], s1[:, :], ACT.Ln).then_inc(nkln_done, 1)
                act.wait_ge(nkln_done, g + 1)
                nc.scalar.activation(nk[:, :], nk[:, :], ACT.Exp, scale=0.5).then_inc(nk_done, 1)

            def take_kq(g):
                act.wait_ge(kk_done, g + 1)
                for hf in range(2):
                    pairs = bank[hf][:, :].rearrange("p (t a i) -> p t a i", a=2, i=P)
                    act.wait_ge(a_chain, g * 4 + 4)
                    nc.scalar.copy(qk[:, 2 * hf:2 * hf + 2, :], pairs[:, :, 1, :]).then_inc(qk_copied, 1)

            decay(0)
            evac(0, 2)
            silu_kq(0)
            square_q(0)
            evac(0, 3)
            take_keys(0)
            act.preload_act_table_set(NLE_SET)
            key_length(0)
            take_kq(0)

            def round_unit(n, slot, src, loaded=None, loads=None):
                if loaded is not None:
                    act.wait_ge(loaded, loads)
                act.wait_ge(units_used, n - (RING - 1))
                nc.scalar.copy(whi[slot][:, 0:src.shape[1], :], src).then_inc(hi_ready, 1)

            def round_out(p):
                tile, src, loads = out_source(p)
                round_unit(U_OUT + p, p % RING, src, wo_in[tile % 4], loads)

            def round_o(k):
                act.wait_ge(fin_done, k + 1)
                nc.scalar.copy(o_hi[:, k, :], ost[:, k, :]).then_inc(o_hi_ready, 1)

            def round_part(name):
                if name[0] == "u":
                    round_out(int(name[1:]))
                else:
                    if name == "h0":
                        act.wait_ge(units_used, U_OUT)
                    round_o(int(name[1:]))

            def delta_rule(g, last):
                plan = FILL_LAST if last else FILL
                taken = [0]

                def round_beside(step):
                    if last:
                        for name in ROUNDED.get(step, ()):
                            round_part(name)

                def evac_before(step):
                    done = min(slices_before(plan, step), Z_SLICES if last else 48) // KD
                    while taken[0] < done:
                        u = taken[0]
                        if u < 2:
                            if last:
                                act.wait_ge(fin_done, g * 2)
                            act.wait_ge(units_used, g * UNITS_GROUP + 2 * (u + 5))
                            nc.scalar.activation(sz[:, u, :], bank[6 + u][:, :], ACT.Silu).then_inc(zsilu_done, 1)
                        else:
                            evac(g + 1, u - 2)
                        taken[0] += 1

                for a in range(2):
                    act.wait_ge(a_done, g * 2 + a + 1)
                    nc.scalar.copy(yr[:, a, :, 1, :], amat[:, a, :, :]).then_inc(ar_done, 1)
                for i, lv in enumerate(LEVELS):
                    evac_before(f"p{lv}")
                    round_beside(f"p{lv}")
                    if i == V_SILU_LEVEL:
                        for a in range(2):
                            act.wait_ge(vconv_done, g * 2 + a + 1)
                            nc.scalar.activation(va[:, a, :], va[:, a, :], ACT.Silu).then_inc(vsilu_done, 1)
                    lo_half, hi_half = (1 if i == 0 else 0), (1 if i == nl - 1 else 2)
                    for a in range(2):
                        act.wait_ge(yr_done, g * (2 * nl) + 2 * i + a + 1)
                        for hf in range(2):
                            pair = bank[2 + 2 * a + hf][:, :].rearrange("p (t k i) -> p t k i", k=2, i=P)
                            op = nc.scalar.copy(yr[:, a, 2 * hf:2 * hf + 2, lo_half:hi_half, :],
                                                pair[:, :, lo_half:hi_half, :])
                        op.then_inc(yr_copied, 1)
                evac_before("t")
                round_beside("t")
                for a in range(2):
                    act.wait_ge(xt_done, g * 2 + a + 1)
                    nc.scalar.copy(xmat[:, a, :, :], b4[a][:, :, :]).then_inc(x_copied, 1)
                round_beside("r")
                evac_before("f")
                for t in range(NT):
                    evac_before(f"z{t}")
                    act.wait_ge(z_done, g * NT + t + 1)
                    nc.scalar.copy(zbuf[:, :, :].rearrange("p a i -> p (a i)"), bank[1][:, 0:2 * P]).then_inc(z_copied, 1)
                    round_beside(f"z{t}")
                if not last:
                    silu_kq(g + 1)
                act.preload_act_table_set(NLE_SET)
                if not last:
                    take_keys(g + 1)
                act.wait_ge(o_done, g + 1)
                for a in range(2):
                    nc.scalar.activation(osq[:, a, :], bank[4 + a][:, :], ACT.Square).then_inc(osq_done, 1)
                round_beside("kn")
                if not last:
                    decay(g + 1)
                evac_before("kn")
                if not last:
                    act.wait_ge(osum_done, g * 2 + 2)
                    square_q(g + 1)
                    key_length(g + 1)
                for a in range(2):
                    act.wait_ge(oss_done, g * 2 + a + 1)
                    nc.scalar.activation(rstd[:, a, :], bank[2 + a][:, :], ACT.Ln, bias=biases[:, B_QEPS:B_QEPS + 1],
                                         scale=1.0 / P).then_inc(oln_done, 1)
                for a in range(2):
                    act.wait_ge(oln_done, g * 2 + a + 1)
                    nc.scalar.activation(rstd[:, a, :], rstd[:, a, :], ACT.Exp, scale=-0.5).then_inc(rstd_done, 1)
                if not last:
                    evac_before("kk")
                    take_kq(g + 1)
                evac_before("end")

            with act.Fori(0, GROUPS - 1) as g:
                delta_rule(g, False)
            delta_rule(GROUPS - 1, True)

            for name in ROUNDED_LATER:
                round_part(name)

            def round_ffn(n0, half, m, loads=None):
                up, f, hf = (m // 2) % 2, m // 4, m % 2
                need = loads if m in (0, 2) else None
                round_unit(n0 + m, m % RING, wraw[2 * half + up][:, HALF * hf:HALF * hf + HALF, f * P:(f + 1) * P],
                           wf_in[2 * half + up] if need is not None else None, need)

            def take_x1(c):
                act.wait_ge(x1_done, c + 1)
                if c >= 3:
                    act.wait_ge(x1add_done, c - 2)
                nc.scalar.activation(sq[:, c % 2 if c else 2, :], xt[:, c, :], ACT.Square).then_inc(x1sq_done, 1)
                nc.scalar.activation(h2_hi[:, c, :], xt[:, c, :], ACT.Copy, scale=ffnw[:, c:c + 1]).then_inc(h2_hi_ready, 1)

            for c in range(4):
                round_out(16 + c)
                take_x1(c)
            for c in range(4, KD):
                for q in range(4):
                    if c < KD - 1:
                        round_out(4 * (c + 1) + q)
                    else:
                        round_ffn(U_FFN, 0, q, 16)
                take_x1(c)
            act.wait_ge(x1ss_done, 1)
            nc.scalar.activation(rstd2[:, :], bank[5][:, :], ACT.Ln, bias=biases[:, B_EPS:B_EPS + 1], scale=1.0 / D).then_inc(x1ln_done, 1)
            act.wait_ge(x1ln_done, 1)
            nc.scalar.activation(rstd2[:, :], rstd2[:, :], ACT.Exp, scale=-0.5).then_inc(rstd2_done, 1)

            def ffn_pair(f0, n0, half, next_loads):
                for f in range(2):
                    for q in range(4):
                        if q == 2:
                            act.wait_ge(gs_done, f0 + (f + 1))
                            nc.scalar.activation(tmp[:, f, :], tmp[:, f, :], ACT.Silu).then_inc(sg_done, 1)
                        if f == 0:
                            round_ffn(n0, half, 4 + q)
                        elif next_loads is not None:
                            round_ffn(n0 + 8, 1 - half, q, next_loads)
                        else:
                            round_down(0, 0, q)
                    act.wait_ge(prod2_done, f0 + (f + 1))
                    nc.scalar.copy(act_hi[:, bass.ds(f0 + f, 1), :].squeeze(1), tmp[:, f, :]).then_inc(act_hi_ready, 1)

            def round_down(c, s, q):
                k = sum(DOWN_K[:q])
                round_unit(U_DOWN + 4 * c + q, q, wdown_raw[s][:, k:k + DOWN_K[q], :],
                           wd_in[s] if q == 0 else None, 16 * (c // 2 + 1))

            with act.Fori(0, 5) as i:
                ffn_pair(i * 4, i * 16 + U_FFN, 0, i * 16 + 16)
                ffn_pair(i * 4 + 2, i * 16 + (U_FFN + 8), 1, i * 16 + 32)
            ffn_pair(20, U_FFN + 80, 0, None)

            def take_x2(c):
                act.wait_ge(x2_done, c + 1)
                if c >= 2:
                    if c >= 3:
                        act.wait_ge(x2add_done, c - 2)
                    act.wait_ge(yt_in_bank, c - 1)
                else:
                    act.wait_ge(act_lo_ready, KF)
                nc.scalar.activation(tmp[:, c % 2, :] if c else x2sum, xt[:, c, :], ACT.Square).then_inc(x2sq_done, 1)
                nc.scalar.activation(yw[:, c % 2, :], xt[:, c, :], ACT.Copy, scale=finw[:, c:c + 1]).then_inc(yw_done, 1)

            for c in range(KD):
                if c < KD - 1:
                    for q in range(4):
                        round_down(c + 1, (c + 1) % 2, q)
                if c == 4:
                    act.wait_ge(yt_in_bank, 4)
                    for t in range(NT):
                        nc.scalar.copy(ytok[:, t, 0:T], bank[t][:, :]).then_inc(yt_copied, 1)
                if c == KD - 1:
                    act.preload_act_table_set(NLE_SET)
                take_x2(c)
            act.wait_ge(x2ss_done, 2)
            nc.scalar.activation(rstd3[:, :], bank[5][:, 0:NT], ACT.Ln, bias=biases[:, B_EPS:B_EPS + 1], scale=1.0 / D).then_inc(x2ln_done, 1)
            act.wait_ge(x2ln_done, 1)
            nc.scalar.activation(rstd3[:, :], rstd3[:, :], ACT.Exp, scale=-0.5).then_inc(rstd3_done, 1)
            act.wait_ge(rstd3_done, 1)
            act.wait_ge(yt_in_bank, KD)
            for t in range(2):
                nc.scalar.activation(ytok[:, t, T:2 * T], bank[t][:, :], ACT.Copy, scale=rstd3[:, t:t + 1]).then_inc(y_done[t], 1)

        @block.vector
        def _(dve):
            dve.wait_ge(rs_ready, 1)
            for t in range(NT):
                nc.vector.tensor_scalar(xn[:, t, :], xs[:, t, :], rs[:, t:t + 1], None, ALU.mult).then_inc(xn_ready, 1)
            dve.wait_ge(vec_done, 1)
            for k in range(KD):
                dve.wait_ge(h_hi_ready, k + 1)
                nc.vector.scalar_tensor_tensor(out=h_lo[:, k, :], in0=bank[k % 4][:, :], scalar=mixw[:, k:k + 1],
                                               in1=h_hi[:, k, :].bitcast(F32), op0=ALU.mult,
                                               op1=ALU.subtract).then_inc(h_lo_ready, 1)
            dve.wait_ge(small_in, 96)
            dve.wait_ge(gate_act, 2)
            nc.vector.tensor_tensor(yt[:, :, :], b4[4][:, :, P - 16:P], dtb[:, :].unsqueeze(1).to_broadcast([P, NT, HEADS]),
                                    ALU.add).then_inc(gate_dve, 1)
            dve.wait_ge(gate_dve, 1)
            nc.vector.scalar_tensor_tensor(out=ab[:, :, :], in0=yt[:, :, :], scalar=-1.0, in1=yt[:, :, :],
                                           op0=ALU.mult, op1=ALU.max).then_inc(gate_dve, 1)
            nc.vector.tensor_scalar(bt[:, :, :], bt[:, :, :], 1.0, None, ALU.add).then_inc(gate_dve, 1)
            dve.wait_ge(gate_dve, 3)
            by_head = [gates[:, k, :, :].rearrange("p h t -> p t h") for k in range(6)]
            flat = [gates[:, k, :, :].rearrange("p h t -> p (h t)") for k in range(6)]
            nc.vector.reciprocal(by_head[K_BETA], bt[:, :, :]).then_inc(gate_dve, 1)
            dve.wait_ge(gate_act, 4)
            nc.vector.scalar_tensor_tensor(out=sp_[:, :, :], in0=yt[:, :, :], scalar=0.0, in1=ab[:, :, :],
                                           op0=ALU.max, op1=ALU.add).then_inc(gate_dve, 1)
            dve.wait_ge(gate_dve, 5)
            nc.vector.scalar_tensor_tensor(out=by_head[K_G], in0=sp_[:, :, :], scalar=-1.0,
                                           in1=ealog[:, :].unsqueeze(1).to_broadcast([P, NT, HEADS]),
                                           op0=ALU.mult, op1=ALU.mult).then_inc(gate_dve, 1)
            dve.wait_ge(gate_act, 6)
            nc.vector.tensor_copy(flat[K_GC], bank[5][:, 0:HEADS * NT]).then_inc(gate_dve, 1)
            nc.vector.tensor_scalar(flat[K_NEG_EGC], flat[K_NEG_EGC], -1.0, None, ALU.mult).then_inc(gate_dve, 1)
            dve.wait_ge(gate_dve, 7)
            nc.vector.tensor_tensor(gl_gc[:, :], bank[5][:, HEADS * NT:2 * HEADS * NT], flat[K_GC],
                                    ALU.subtract).then_inc(gate_dve, 1)
            for k in range(2):
                nc.vector.tensor_copy(gc_twice[:, k, :], bank[5][:, 0:HEADS * NT]).then_inc(gc_twice_made, 1)
            dve.wait_ge(gc_first_made, 2)
            half = HEADS * NT
            nc.vector.tensor_tensor(gc_parts[half:P, :], bank[5][half:P, P:2 * P], gc_first[half:P, :].bitcast(F32),
                                    ALU.subtract).then_inc(gc_parts_made, 1)
            nc.vector.tensor_tensor(pick[:, :], ident[:, 0:half], ident[:, half:P], ALU.add).then_inc(pick_made, 1)
            dve.wait_ge(gc_parts_made, 1)
            dve.wait_ge(pick_made, 1)
            dve.wait_ge(gate_act, 7)
            dve.wait_ge(xt_copied, KD)
            nc.vector.memset(raw[:, :, 0:PADC], 0.0).then_inc(pad_set, 1)
            dve.wait_ge(gate_dve, 9)

            def take_taps(g):
                nc.vector.tensor_copy(cwg[:, :, :], cw[:, bass.ds(g, 1), :, :].squeeze(1)).then_inc(cwg_done, 1)
                dve.wait_ge(cwg_done, g + 1)

            def take_scalars(g):
                nc.vector.tensor_copy(pickg[:, :, :].rearrange("p a t -> p (a t)"),
                                      pick[:, bass.ds(g * 2 * NT, 2 * NT)])
                nc.vector.tensor_copy(gg[:, :, :, :], gates[:, :, bass.ds(g * 2, 2), :]).then_inc(gg_done, 1)
                dve.wait_ge(gg_done, g + 1)

            def convolve(g, j, n, tiles, accs, step, done):
                u, acc = tiles[n], accs[n]
                src = raw[:, u, j:j + T].rearrange("p (t i) -> p t i", i=P)
                if j == CONV - 1:
                    dve.wait_ge(evac_done, g * 4 + (u + 1))
                    nc.vector.tensor_scalar(acc, src, cwg[:, u, j:j + 1], None, ALU.mult).then_inc(step, 1)
                else:
                    dve.wait_ge(step, g * 6 + 2 * (CONV - 2 - j) + n + 1)
                    nc.vector.scalar_tensor_tensor(out=acc, in0=src, scalar=cwg[:, u, j:j + 1], in1=acc,
                                                   op0=ALU.mult, op1=ALU.add).then_inc(done if j == 0 else step, 1)

            kq_acc = (dcmat[:, 0, :, :], dcmat[:, 1, :, :])
            v_acc = tuple(va[:, a, :].rearrange("p (t i) -> p t i", i=P) for a in range(2))

            def convolve_kq(g, j, n):
                convolve(g, j, n, (1, 0), kq_acc, conv_step, conv_done)

            def convolve_v(g, j):
                for n in range(2):
                    convolve(g, j, n, (2, 3), v_acc, vconv_step, vconv_done)

            def exponents(g):
                for a in range(2):
                    dve.wait_ge(bc_done, g * 2 + a + 1)
                    for t in range(NT):
                        op = nc.vector.tensor_scalar(dmat[:, a, t, :], b4[a][:, t, :], gg[:, K_GC, a, t:t + 1], 0.0,
                                                     ALU.subtract, ALU.min)
                    op.then_inc(arg_done, 1)

            def column_factors(g):
                dve.wait_ge(ksq_done, g * 4 + 4)
                nc.vector.tensor_scalar(s1[:, :], ksum[:, :], EPS, None, ALU.add).then_inc(s1_done, 1)
                dve.wait_ge(s1_done, g + 1)
                nc.vector.reciprocal(rc[:, :], s1[:, :]).then_inc(c_chain, 1)
                dve.wait_ge(c_chain, g * 3 + 1)
                nc.vector.tensor_tensor(cc[:, :, :], gg[:, K_BETA, :, :], rc[:, :].unsqueeze(1).to_broadcast([P, 2, NT]),
                                        ALU.mult).then_inc(c_chain, 1)
                dve.wait_ge(c_chain, g * 3 + 2)
                nc.vector.tensor_tensor(cd[:, :, :], cc[:, :, :], gg[:, K_DEC, :, :], ALU.mult).then_inc(c_chain, 1)

            def decay_times_c(g):
                dve.wait_ge(silu_done, g * 2 + 2)
                for a in range(2):
                    dve.wait_ge(dexp_done, g * 2 + a + 1)
                    for t in range(NT):
                        nc.vector.scalar_tensor_tensor(out=dcmat[:, a, t, :], in0=dmat[:, a, t, :], scalar=cc[:, a, t:t + 1],
                                                       in1=cst[:, STRICT, :], op0=ALU.mult, op1=ALU.mult).then_inc(dc_done, 1)

            def unit_plus_n(g):
                dve.wait_ge(kk_done, g + 1)
                for a in range(2):
                    dve.wait_ge(dc_done, g * 8 + 4 * a + 4)
                    for hf in range(2):
                        pairs = bank[hf][:, :].rearrange("p (t a i) -> p t a i", a=2, i=P)
                        nc.vector.tensor_tensor(amat[:, a, 2 * hf:2 * hf + 2, :], pairs[:, :, 0, :],
                                                dcmat[:, a, 2 * hf:2 * hf + 2, :], ALU.mult).then_inc(a_chain, 1)
                for a in range(2):
                    dve.wait_ge(a_chain, g * 4 + 2 * a + 2)
                    nc.vector.tensor_tensor(amat[:, a, :, :], amat[:, a, :, :], over_tiles(IDENT), ALU.add).then_inc(a_done, 1)

            take_taps(0)
            take_scalars(0)
            exponents(0)
            for j in range(CONV - 1, -1, -1):
                for n in range(2):
                    convolve_kq(0, j, n)
            column_factors(0)
            decay_times_c(0)
            unit_plus_n(0)

            def delta_rule(g, last):
                convolve_v(g, 3)

                def between_levels(i):
                    if i == 0:
                        for a in range(2):
                            dve.wait_ge(a_done, g * 2 + a + 1)
                            nc.vector.tensor_tensor(yr[:, a, :, 0, :], amat[:, a, :, :], over_tiles(PAIR), ALU.mult).then_inc(y1_done, 1)
                    elif i < 4:
                        convolve_v(g, 3 - i)
                    elif i == 4:
                        dve.wait_ge(ktok_copied, g + 1)
                        dve.wait_ge(c_chain, g * 3 + 3)
                        for a in range(2):
                            nc.vector.tensor_tensor(kdec[:, a, :, :], ktok[:, :, :], per_token(cd[:, a, :]),
                                                    ALU.mult).then_inc(kdec_done, 1)
                    elif i == 5:
                        for a in range(2):
                            nc.vector.tensor_tensor(qhat[:, a, :, :], qhat[:, a, :, :], kq[:, :, 1, :], ALU.mult).then_inc(qhat_done, 1)
                        if not last:
                            dve.wait_ge(vconv_done, g * 2 + 2)
                            take_taps(g + 1)

                for i, lv in enumerate(LEVELS):
                    for a in range(2):
                        dve.wait_ge(p_done, g * (2 * nl) + 2 * i + a + 1)
                        if i > 0:
                            dve.wait_ge(yr_done, g * (2 * nl) + 2 * (i - 1) + a + 1)
                        nc.vector.tensor_tensor(pmat[:, a, :, :], b4[a][:, :, :], over_tiles(LEVEL0 + i), ALU.mult).then_inc(pm_done, 1)
                    between_levels(i)
                dve.wait_ge(a_chain, g * 4 + 4)
                for a in range(2):
                    for t in range(NT):
                        nc.vector.scalar_tensor_tensor(out=dcmat[:, a, t, :], in0=ident, scalar=cc[:, a, t:t + 1],
                                                       in1=dcmat[:, a, t, :], op0=ALU.mult,
                                                       op1=ALU.add).then_inc(dg_done, 1)
                dve.wait_ge(qk_copied, g * 2 + 2)
                for a in range(2):
                    dve.wait_ge(dg_done, g * 8 + 4 * a + 4)
                    nc.vector.tensor_tensor(attn[:, a, :, :], qk[:, :, :], dcmat[:, a, :, :], ALU.mult).then_inc(attn_done, 1)
                for a in range(2):
                    dve.wait_ge(res_done, g * 2 + a + 1)
                    nc.vector.scalar_tensor_tensor(out=fmat[:, a, :, :], in0=b4[a][:, :, :], scalar=-1.0, in1=over_tiles(IDENT),
                                                   op0=ALU.mult, op1=ALU.add).then_inc(f_done, 1)
                dve.wait_ge(nk_done, g + 1)
                for a in range(2):
                    dve.wait_ge(vt_done, g * 2 + 2)
                    nc.vector.tensor_tensor(vn[:, a, :, :], b4[2 + a][:, :, :], per_token(nk[:, :]), ALU.mult).then_inc(vn_done, 1)
                for a in range(2):
                    dve.wait_ge(yf_done, g * 2 + a + 1)
                    nc.vector.tensor_tensor(yfin[:, a, :, :], b4[4 + a][:, :, :], yr[:, a, :, 0, :].bitcast(F32),
                                            ALU.add).then_inc(yf_added, 1)
                for t in range(NT):
                    if t > 0:
                        dve.wait_ge(ks_done, g * 3 + t)
                        for a in range(2):
                            nc.vector.scalar_tensor_tensor(out=rbuf[:, a, :], in0=bank[0][:, a * P:(a + 1) * P],
                                                           scalar=gg[:, K_NEG_EGC, a, t:t + 1], in1=vn[:, a, t, :],
                                                           op0=ALU.mult, op1=ALU.add).then_inc(r_done, 1)
                    if t == 0:
                        dve.wait_ge(attn_done, g * 2 + 2)
                    if not last:
                        convolve_kq(g + 1, CONV - 1 - t, 0)
                    if t < NT - 1:
                        dve.wait_ge(sn_done, g * 3 + t + 1)
                        for a in range(2):
                            new = bank[2][:, a * P:(a + 1) * P]
                            if t == 0:
                                nc.vector.tensor_copy(state[:, a, :], new).then_inc(s_done, 1)
                            else:
                                nc.vector.scalar_tensor_tensor(out=state[:, a, :], in0=state[:, a, :],
                                                               scalar=gg[:, K_EGL, a, t:t + 1], in1=new,
                                                               op0=ALU.mult, op1=ALU.add).then_inc(s_done, 1)
                    if not last:
                        convolve_kq(g + 1, CONV - 1 - t, 1)
                if not last:
                    dve.wait_ge(r_done, g * 6 + 6)
                    take_scalars(g + 1)
                if not last:
                    exponents(g + 1)
                for a in range(2):
                    dve.wait_ge(osq_done, g * 2 + a + 1)
                    nc.vector.scalar_tensor_tensor(out=osq[:, a, :], in0=qsq[:, :], scalar=EPS * P * P, in1=osq[:, a, :],
                                                   op0=ALU.mult, op1=ALU.add).then_inc(osum_done, 1)
                if not last:
                    column_factors(g + 1)
                    decay_times_c(g + 1)
                    unit_plus_n(g + 1)
                for a in range(2):
                    dve.wait_ge(rstd_done, g * 2 + a + 1)
                    nc.vector.scalar_tensor_tensor(out=rstd[:, a, :], in0=bank[4 + a][:, :], scalar=nw, in1=rstd[:, a, :],
                                                   op0=ALU.mult, op1=ALU.mult).then_inc(of_made, 1)
                for a in range(2):
                    dve.wait_ge(of_made, g * 2 + a + 1)
                    dve.wait_ge(zsilu_done, g * 2 + a + 1)
                    nc.vector.tensor_tensor(ost[:, bass.ds(g * 2 + a, 1), :].squeeze(1), rstd[:, a, :], sz[:, a, :],
                                            ALU.mult).then_inc(fin_done, 1)

            with dve.Fori(0, GROUPS - 1) as g:
                delta_rule(g, False)
            delta_rule(GROUPS - 1, True)

            for c in range(KD):
                dve.wait_ge(units_used, U_OUT + 13 + c if c < 4 else U_OUT + 4 * (c + 1))
                nc.vector.tensor_tensor(xt[:, c, :], bank[OUT_BANK[c]][:, :], xt[:, c, :], ALU.add).then_inc(x1_done, 1)
                dve.wait_ge(h2_hi_ready, c + 1)
                nc.vector.scalar_tensor_tensor(out=h2_lo[:, c, :], in0=xt[:, c, :], scalar=ffnw[:, c:c + 1],
                                               in1=h2_hi[:, c, :].bitcast(F32), op0=ALU.mult,
                                               op1=ALU.subtract).then_inc(h2_lo_ready, 1)
                if 0 < c < KD - 1:
                    dve.wait_ge(x1sq_done, c + 1)
                    if c > 1:
                        dve.wait_ge(x1add_done, c - 1)
                    nc.vector.tensor_tensor(sq[:, 2, :], sq[:, 2, :], sq[:, c % 2, :], ALU.add).then_inc(x1add_done, 1)
            dve.wait_ge(rstd2_done, 1)

            def ffn_pair(f0, n0):
                for f in range(2):
                    dve.wait_ge(units_used, n0 + (4 * f + 2))
                    nc.vector.tensor_tensor(tmp[:, f, :], bank[f][:, :], rstd2[:, :], ALU.mult).then_inc(gs_done, 1)
                    dve.wait_ge(units_used, n0 + (4 * f + 4))
                    dve.wait_ge(sg_done, f0 + (f + 1))
                    nc.vector.tensor_tensor(tmp[:, f, :], bank[2 + f][:, :], tmp[:, f, :], ALU.mult).then_inc(prod_done, 1)
                    dve.wait_ge(prod_done, f0 + (f + 1))
                    nc.vector.tensor_tensor(tmp[:, f, :], tmp[:, f, :], rstd2[:, :], ALU.mult).then_inc(prod2_done, 1)
                    dve.wait_ge(act_hi_ready, f0 + (f + 1))
                    at = bass.ds(f0 + f, 1)
                    nc.vector.tensor_tensor(act_lo[:, at, :].squeeze(1), tmp[:, f, :], act_hi[:, at, :].squeeze(1).bitcast(F32),
                                            ALU.subtract).then_inc(act_lo_ready, 1)

            with dve.Fori(0, 5) as i:
                ffn_pair(i * 4, i * 16 + U_FFN)
                ffn_pair(i * 4 + 2, i * 16 + (U_FFN + 8))
            ffn_pair(20, U_FFN + 80)
            for c in range(KD):
                dve.wait_ge(units_used, U_DOWN + 4 * (c + 1))
                nc.vector.tensor_tensor(xt[:, c, :], bank[6 + c % 2][:, :], xt[:, c, :], ALU.add).then_inc(x2_done, 1)
                if 0 < c < KD - 1:
                    dve.wait_ge(x2sq_done, c + 1)
                    if c > 1:
                        dve.wait_ge(x2add_done, c - 1)
                    nc.vector.tensor_tensor(x2sum, x2sum, tmp[:, c % 2, :], ALU.add).then_inc(x2add_done, 1)
            dve.wait_ge(rstd3_done, 1)
            for t in range(NT):
                nc.vector.tensor_scalar(ytok[:, t, 0:T], ytok[:, t, 0:T], rstd3[:, t:t + 1], None, ALU.mult).then_inc(y_done[t], 1)
            dve.wait_ge(yt_in_bank, KD)
            for t in range(2, NT):
                nc.vector.tensor_scalar(ytok[:, t, T:2 * T], bank[t][:, :], rstd3[:, t:t + 1], None, ALU.mult).then_inc(y_done[t], 1)


INPUTS = ("x", "gdn_w_in", "gdn_conv_w", "gdn_a_log", "gdn_dt_bias", "gdn_norm_w", "gdn_w_out",
          "mix_norm_w", "ffn_norm_w", "ffn_w_gate", "ffn_w_up", "ffn_w_down")


def kernel(**inputs):
    import concourse.bacc as bacc
    from concourse.bass_utils import run_bass_kernel_spmd

    nc = bacc.Bacc("TRN2", target_bir_lowering=False, num_devices=1)
    arrays = {name: np.ascontiguousarray(np.asarray(inputs[name])[0]) for name in INPUTS}
    arrays["final_norm_w"] = np.ascontiguousarray(inputs["final_norm_w"])
    arrays["shape_constants"] = shape_constants()
    args = [nc.dram_tensor(f"in_{name}", a.shape, F32, kind="ExternalInput").ap() for name, a in arrays.items()]
    result = nc.dram_tensor("result", (T, D), F32, kind="ExternalOutput").ap()
    build(nc, *args, result)
    r = run_bass_kernel_spmd(nc, [{f"in_{name}": a for name, a in arrays.items()}], core_ids=[0])
    return r.results[0]["result"].reshape(1, T, D)
```
